# Optimizing a Trainium2 kernel written in Bass

```python
import math
import jax, jax.numpy as jnp
from jax import lax
import numpy as np

D_MODEL = 1024
BATCH = 1
SEQ = 128
DEPTH = 2
DEC_BATCH = 1
DEC_SEQ = 512
PAST_LEN = 128

GRID_W = 64
BR_W = 512
HY_W = BR_W
HY_EMB = 33
HY_BANDS = (HY_EMB - 1) // 2
HY_FFN = 64
HY_MAX_DECAY = math.log(1e-2) / 0.3
HY_MIN_DECAY = math.log(1e-2) / 1.5
RW_N = 64
RW_H = BR_W // RW_N
RW_W = RW_H * RW_N
W_LORA = 64
A_LORA = 64
RW_DECAY_SCALE = math.exp(-0.5)
RW_GN_EPS = 64e-5
DA_DH = 64
DA_H = BR_W // (2 * DA_DH)
DA_QW = DA_H * 2 * DA_DH
DA_VW = DA_H * 2 * DA_DH
ROPE_AXIS = DA_DH // 2
ROPE_BASE = 10000.0
Q_BLOCK = 128
NORM_EPS = 1e-6
N_BRANCH = 3
RW_SHIFT_W = 3 * RW_W + 2 * W_LORA + 2 * A_LORA
IN_SIZES = (3 * HY_W, HY_W, RW_SHIFT_W, RW_W, DA_QW, DA_QW, DA_VW, DA_VW, N_BRANCH * D_MODEL)
N_IN = sum(IN_SIZES)
IN_SPLITS = tuple(int(s) for s in np.cumsum(IN_SIZES)[:-1])

kernel_name = "hyena_rwkv7_diffattn_prefix_dit"

F32 = jnp.float32

def _rmsnorm(x, g, eps=NORM_EPS):
    xf = x.astype(F32)
    y = xf * lax.rsqrt(jnp.mean(xf * xf, axis=-1, keepdims=True) + eps)
    return (y * g.astype(F32)).astype(x.dtype)

def _centred_conv3(u, w, b):
    up = jnp.pad(u, ((0, 0), (1, 1), (0, 0)))
    return up[:, :-2] * w[0] + up[:, 1:-1] * w[1] + up[:, 2:] * w[2] + b

def _hyena_filters(L, f1, fb1, freq, f2, fb2, f3):
    t = jnp.linspace(0.0, 1.0, L, dtype=F32)[:, None]
    w = 2.0 * math.pi * jnp.arange(L, dtype=F32)[:, None] / L
    bands = jnp.linspace(1e-4, HY_BANDS - 1, HY_BANDS, dtype=F32)[None, :]
    z = jnp.concatenate([t, jnp.cos(bands * w), -jnp.sin(bands * w)], axis=-1)
    freq = freq.astype(F32)
    hid = jnp.sin(freq * (z @ f1.astype(F32) + fb1.astype(F32)))
    hid = jnp.sin(freq * (hid @ f2.astype(F32) + fb2.astype(F32)))
    h = hid @ f3.astype(F32)
    deltas = jnp.linspace(HY_MIN_DECAY, HY_MAX_DECAY, HY_W, dtype=F32)
    window = jnp.exp(-t * jnp.abs(deltas)[None, :])
    return h[:, :HY_W] * window, h[:, HY_W:] * window

def _long_conv_bidir(u, h_f, h_b, bias_d):
    L = u.shape[1]
    C = u.shape[2]
    h_full = jnp.concatenate([h_f, jnp.zeros((1, C), F32), h_b[1:][::-1]], axis=0)
    uf = u.astype(F32)
    U = jnp.fft.rfft(uf, n=2 * L, axis=1)
    H = jnp.fft.rfft(h_full, n=2 * L, axis=0)
    y = jnp.fft.irfft(U * H[None], n=2 * L, axis=1)[:, :L]
    return y + uf * bias_d.astype(F32)

def _hyena_branch(z, gate, p):
    u = _centred_conv3(z, p["hy_conv_w"], p["hy_conv_b"])
    v, x1, x2 = jnp.split(u, 3, axis=-1)
    h_f, h_b = _hyena_filters(u.shape[1], p["hy_f1"], p["hy_fb1"], p["hy_freq"],
                              p["hy_f2"], p["hy_fb2"], p["hy_f3"])
    y = x1.astype(F32) * _long_conv_bidir(x2 * v, h_f, h_b, p["hy_bias"])
    return (y * jax.nn.silu(gate.astype(F32))).astype(z.dtype)

def _rwkv_scan(r, w, kk, a, k, v, s0, reverse):
    def step(S, inp):
        r_t, w_t, kk_t, a_t, k_t, v_t = inp
        sa = jnp.einsum('bhvk,bhk->bhv', S, -kk_t)
        S = (S * w_t[:, :, None, :] + sa[..., None] * (kk_t * a_t)[:, :, None, :]
             + v_t[..., None] * k_t[:, :, None, :])
        return S, jnp.einsum('bhvk,bhk->bhv', S, r_t)
    xs = tuple(jnp.moveaxis(t, 1, 0) for t in (r, w, kk, a, k, v))
    S, ys = lax.scan(step, s0.astype(F32), xs, reverse=reverse)
    return jnp.moveaxis(ys, 0, 1), S

def _rwkv_branch(zr, gate, p, s0_f, s0_b):
    B, L, _ = zr.shape
    zr = zr.astype(F32)
    zp = jnp.pad(zr, ((0, 0), (1, 1), (0, 0)))
    nbr = 0.5 * (zp[:, :-2] + zp[:, 2:])
    zr = zr + p["rw_mu"].astype(F32) * (nbr - zr)
    r, k, v, wl, al = jnp.split(zr, [RW_W, 2 * RW_W, 3 * RW_W, 3 * RW_W + 2 * W_LORA], axis=-1)
    wls = jnp.split(wl, 2, axis=-1)
    als = jnp.split(al, 2, axis=-1)
    heads = lambda t: t.reshape(B, L, RW_H, RW_N)
    kk = heads(k * p["rw_kk"].astype(F32))
    kk = kk * lax.rsqrt(jnp.sum(kk * kk, axis=-1, keepdims=True) + 1e-12)
    ys, states, kds = [], [], []
    for d, (s0, rev) in enumerate(((s0_f, False), (s0_b, True))):
        w = jnp.exp(-RW_DECAY_SCALE * jax.nn.sigmoid(
            p["rw_w0"][d].astype(F32) + jnp.tanh(wls[d]) @ p["rw_w2"][d].astype(F32)))
        a = jax.nn.sigmoid(p["rw_a0"][d].astype(F32) + als[d] @ p["rw_a2"][d].astype(F32))
        kd = k * (1.0 + (a - 1.0) * p["rw_ka"].astype(F32))
        y, s = _rwkv_scan(heads(r), heads(w), kk, heads(a), heads(kd), heads(v), s0, rev)
        ys.append(y)
        states.append(s)
        kds.append(kd)
    y = ys[0] + ys[1]
    mu = jnp.mean(y, axis=-1, keepdims=True)
    var = jnp.mean(jnp.square(y - mu), axis=-1, keepdims=True)
    y = ((y - mu) * lax.rsqrt(var + RW_GN_EPS)).reshape(B, L, RW_W)
    y = y * p["rw_ln_w"].astype(F32) + p["rw_ln_b"].astype(F32)
    k_mix = heads(0.5 * (kds[0] + kds[1]))
    bonus = jnp.sum(heads(r) * k_mix * p["rw_rk"].astype(F32), axis=-1, keepdims=True) * heads(v)
    y = (y + bonus.reshape(B, L, RW_W)) * jax.nn.silu(gate.astype(F32))
    return y.astype(gate.dtype), states[0], states[1]

def _rope_axis(x, pos):
    half = ROPE_AXIS // 2
    freqs = ROPE_BASE ** (-jnp.arange(half, dtype=F32) / half)
    ang = pos.astype(F32)[:, None] * freqs[None, :]
    cos = jnp.cos(ang)[None, :, None, None, :]
    sin = jnp.sin(ang)[None, :, None, None, :]
    x1, x2 = x[..., :half], x[..., half:]
    return jnp.concatenate([x1 * cos - x2 * sin, x1 * sin + x2 * cos], axis=-1)

def _rope2d(x):
    L = x.shape[1]
    rows = L // GRID_W
    row = jnp.repeat(jnp.arange(rows), GRID_W)
    col = jnp.tile(jnp.arange(GRID_W), rows)
    xf = x.astype(F32)
    out = jnp.concatenate([_rope_axis(xf[..., :ROPE_AXIS], row),
                           _rope_axis(xf[..., ROPE_AXIS:], col)], axis=-1)
    return out.astype(x.dtype)

def _diff_attention(q, k, v, lam):
    B, Lq, H, _, Dh = q.shape
    nb = Lq // Q_BLOCK
    qb = jnp.moveaxis(q.reshape(B, nb, Q_BLOCK, H, 2, Dh), 1, 0)
    kf = k.astype(F32)
    vf = v.astype(F32)
    scale = Dh ** -0.5

    def block(qi):
        s = jnp.einsum('bqhmd,bkhmd->bhmqk', qi.astype(F32), kf) * scale
        pr = jax.nn.softmax(s, axis=-1)
        pd = pr[:, :, 0] - lam * pr[:, :, 1]
        return jnp.einsum('bhqk,bkhe->bqhe', pd, vf)
    o = lax.map(block, qb)
    return jnp.moveaxis(o, 0, 1).reshape(B, Lq, H, 2 * Dh)

def _diff_branch(q, k, v, gate, p, lam_init, ctx_kv):
    B, L, _ = q.shape
    q = _rmsnorm(q.reshape(B, L, DA_H, 2, DA_DH), p["da_gq"])
    k = _rmsnorm(k.reshape(B, L, DA_H, 2, DA_DH), p["da_gk"])
    v = v.reshape(B, L, DA_H, 2 * DA_DH)
    if ctx_kv is None:
        keys, vals = k, v
    else:
        q = _rope2d(q)
        keys = jnp.concatenate([ctx_kv[0].astype(k.dtype), _rope2d(k)], axis=1)
        vals = jnp.concatenate([ctx_kv[1].astype(v.dtype), v], axis=1)
    lam = (jnp.exp(jnp.sum(p["da_lq1"].astype(F32) * p["da_lk1"].astype(F32)))
           - jnp.exp(jnp.sum(p["da_lq2"].astype(F32) * p["da_lk2"].astype(F32))) + lam_init)
    o = _diff_attention(q, keys, vals, lam)
    o = _rmsnorm(o, p["da_gsub"], 1e-5) * (1.0 - lam_init)
    y = o.reshape(B, L, DA_VW) * jax.nn.silu(gate.astype(F32))
    return y.astype(gate.dtype), k, v

def _layer(x, cvec, p, lam_init, ctx):
    mod = jax.nn.silu(cvec) @ p["w_ada"] + p["b_ada"]
    shift, scale, gate = jnp.split(mod, 3, axis=-1)
    h = _rmsnorm(x, p["norm_g"]) * (1.0 + scale[:, None, :]) + shift[:, None, :]
    z = h @ p["w_in"]
    hy_z, hy_g, rw_z, rw_g, da_q, da_k, da_v, da_g, mg = jnp.split(z, IN_SPLITS, axis=-1)
    if ctx is None:
        s0 = jnp.zeros((x.shape[0], RW_H, RW_N, RW_N), F32)
        s0_f, s0_b, ctx_kv = s0, s0, None
    else:
        ctx_k, ctx_v, s0_f, s0_b = ctx
        ctx_kv = (ctx_k, ctx_v)
    y_a = _hyena_branch(hy_z, hy_g, p)
    y_b, s_f, s_b = _rwkv_branch(rw_z, rw_g, p, s0_f, s0_b)
    y_c, k_c, v_c = _diff_branch(da_q, da_k, da_v, da_g, p, lam_init, ctx_kv)
    g_a, g_b, g_c = jnp.split(jax.nn.sigmoid(mg.astype(F32)), 3, axis=-1)
    merged = (g_a * (y_a @ p["w_br"][0]) + g_b * (y_b @ p["w_br"][1])
              + g_c * (y_c @ p["w_br"][2]))
    out = merged.astype(x.dtype) @ p["w_out"]
    x_new = x + (gate[:, None, :] * out).astype(x.dtype)
    if ctx is None:
        return x_new, (k_c, v_c, jnp.stack([s_f, s_b], axis=1))
    return x_new, None

def setup_inputs(seed: int = 0) -> dict:
    key = jax.random.key(seed)
    ks = iter(jax.random.split(key, 48))
    nrm = lambda shape, s=1.0: jax.random.normal(next(ks), shape, F32) * s
    D = D_MODEL
    return {
        "x_prompt": nrm((BATCH, SEQ, D)),
        "x_sample": nrm((DEC_BATCH, DEC_SEQ, D)),
        "cache_k": nrm((DEC_BATCH, DEPTH, PAST_LEN, DA_H, 2, DA_DH)),
        "cache_v": nrm((DEC_BATCH, DEPTH, PAST_LEN, DA_H, 2 * DA_DH)),
        "state_rwkv": nrm((DEC_BATCH, DEPTH, 2, RW_H, RW_N, RW_N), 0.5),
        "c": nrm((DEC_BATCH, D)),
        "c_ctx": nrm((D,)),
        "norm_g": 1.0 + nrm((DEPTH, D), 0.05),
        "w_ada": nrm((DEPTH, D, 3 * D), 0.02),
        "b_ada": nrm((DEPTH, 3 * D), 0.01),
        "w_in": nrm((DEPTH, D, N_IN), D ** -0.5),
        "hy_conv_w": nrm((DEPTH, 3, 3 * HY_W), 3 ** -0.5),
        "hy_conv_b": nrm((DEPTH, 3 * HY_W), 0.01),
        "hy_f1": nrm((DEPTH, HY_EMB, HY_FFN), HY_EMB ** -0.5),
        "hy_fb1": nrm((DEPTH, HY_FFN), 0.1),
        "hy_freq": 1.0 + nrm((DEPTH, HY_FFN), 0.05),
        "hy_f2": nrm((DEPTH, HY_FFN, HY_FFN), HY_FFN ** -0.5),
        "hy_fb2": nrm((DEPTH, HY_FFN), 0.1),
        "hy_f3": nrm((DEPTH, HY_FFN, 2 * HY_W), 0.05 * HY_FFN ** -0.5),
        "hy_bias": nrm((DEPTH, HY_W), 0.1),
        "rw_mu": jax.random.uniform(next(ks), (DEPTH, RW_SHIFT_W), F32),
        "rw_w0": nrm((DEPTH, 2, RW_W), 0.5),
        "rw_w2": nrm((DEPTH, 2, W_LORA, RW_W), W_LORA ** -0.5),
        "rw_a0": nrm((DEPTH, 2, RW_W), 0.5),
        "rw_a2": nrm((DEPTH, 2, A_LORA, RW_W), 0.5 * A_LORA ** -0.5),
        "rw_kk": 0.85 + nrm((DEPTH, RW_W), 0.05),
        "rw_ka": 1.0 + nrm((DEPTH, RW_W), 0.05),
        "rw_rk": nrm((DEPTH, RW_H, RW_N), 0.1),
        "rw_ln_w": 1.0 + nrm((DEPTH, RW_W), 0.05),
        "rw_ln_b": nrm((DEPTH, RW_W), 0.01),
        "da_gq": 1.0 + nrm((DEPTH, DA_DH), 0.05),
        "da_gk": 1.0 + nrm((DEPTH, DA_DH), 0.05),
        "da_lq1": nrm((DEPTH, DA_DH), 0.1),
        "da_lk1": nrm((DEPTH, DA_DH), 0.1),
        "da_lq2": nrm((DEPTH, DA_DH), 0.1),
        "da_lk2": nrm((DEPTH, DA_DH), 0.1),
        "da_gsub": 1.0 + nrm((DEPTH, 2 * DA_DH), 0.05),
        "w_br": nrm((DEPTH, N_BRANCH, BR_W, D), BR_W ** -0.5),
        "w_out": nrm((DEPTH, D, D), D ** -0.5),
    }

def reference(x_prompt, x_sample, cache_k, cache_v, state_rwkv, c, c_ctx,
              norm_g, w_ada, b_ada, w_in, hy_conv_w, hy_conv_b, hy_f1, hy_fb1, hy_freq,
              hy_f2, hy_fb2, hy_f3, hy_bias, rw_mu, rw_w0, rw_w2, rw_a0, rw_a2, rw_kk, rw_ka,
              rw_rk, rw_ln_w, rw_ln_b, da_gq, da_gk, da_lq1, da_lk1, da_lq2, da_lk2, da_gsub,
              w_br, w_out):
    def layer_params(l):
        return dict(norm_g=norm_g[l], w_ada=w_ada[l], b_ada=b_ada[l], w_in=w_in[l],
                    hy_conv_w=hy_conv_w[l], hy_conv_b=hy_conv_b[l], hy_f1=hy_f1[l], hy_fb1=hy_fb1[l],
                    hy_freq=hy_freq[l], hy_f2=hy_f2[l], hy_fb2=hy_fb2[l], hy_f3=hy_f3[l],
                    hy_bias=hy_bias[l], rw_mu=rw_mu[l], rw_w0=rw_w0[l], rw_w2=rw_w2[l],
                    rw_a0=rw_a0[l], rw_a2=rw_a2[l], rw_kk=rw_kk[l], rw_ka=rw_ka[l], rw_rk=rw_rk[l],
                    rw_ln_w=rw_ln_w[l], rw_ln_b=rw_ln_b[l], da_gq=da_gq[l], da_gk=da_gk[l],
                    da_lq1=da_lq1[l], da_lk1=da_lk1[l], da_lq2=da_lq2[l], da_lk2=da_lk2[l],
                    da_gsub=da_gsub[l], w_br=w_br[l], w_out=w_out[l])

    c_prompt = jnp.broadcast_to(c_ctx, (x_prompt.shape[0], D_MODEL))
    xp = x_prompt
    new_k, new_v, new_s = [], [], []
    for l in range(DEPTH):
        lam_init = 0.8 - 0.6 * math.exp(-0.3 * l)
        xp, (k_l, v_l, s_l) = _layer(xp, c_prompt, layer_params(l), lam_init, None)
        new_k.append(k_l)
        new_v.append(v_l)
        new_s.append(s_l)
    new_cache_k = jnp.stack(new_k, axis=1)
    new_cache_v = jnp.stack(new_v, axis=1)
    new_state_rwkv = jnp.stack(new_s, axis=1)

    xs = x_sample
    for l in range(DEPTH):
        lam_init = 0.8 - 0.6 * math.exp(-0.3 * l)
        ctx = (cache_k[:, l], cache_v[:, l], state_rwkv[:, l, 0], state_rwkv[:, l, 1])
        xs, _ = _layer(xs, c, layer_params(l), lam_init, ctx)
    return (xp, xs, new_cache_k, new_cache_v, new_state_rwkv)


_drawn_inputs = setup_inputs


def setup_inputs(seed=0):
    import zlib

    import numpy as np

    out = dict(_drawn_inputs(seed))
    spreads = {}
    factors = {'cache_k': 3.151,
     'cache_v': 2.771,
     'state_rwkv': 4.583,
     'hy_conv_b': 31.456,
     'hy_fb1': 3.686,
     'hy_freq': 8.0,
     'hy_fb2': 3.453,
     'rw_ln_w': 4.988,
     'rw_ln_b': 23.093,
     'da_gq': 8.0,
     'da_lq1': 5.287,
     'da_lk1': 7.962,
     'da_lq2': 6.236,
     'da_lk2': 7.787,
     'da_gsub': 6.472}
    for name, (base, spread) in spreads.items():
        noise = np.random.default_rng([zlib.crc32(name.encode()), seed]).standard_normal(out[name].shape)
        drawn = base * np.exp(spread * noise) if base else spread * noise
        out[name] = __import__('jax').numpy.asarray(drawn.astype(out[name].dtype))
    for name, factor in factors.items():
        out[name] = (out[name] * factor).astype(out[name].dtype)
    return out
```

```python
import math
from contextlib import ExitStack

import numpy as np
import concourse.bass as bass
from concourse import mybir

F32 = mybir.dt.float32
I32 = mybir.dt.int32
ALU = mybir.AluOpType
ACT = mybir.ActivationFunctionType
AX = mybir.AxisListType

DEPTH, D, S, P, PAST = 2, 1024, 512, 128, 128
T = S + P
KD = D // 128
BR = 512
JT = BR // 128
NT = T // 128
HEADS = 4
DH = 64
GRID_W = 64
HY_EMB = 33
DECAY = math.exp(-0.5)
KAPPA = -0.5 * DECAY
TWO_PI = 2.0 * math.pi
ROUND = 12582912.0
PI_HI, PI_MID = 6.28125, 0.0019350051879882812
PI_LO = TWO_PI - PI_HI - PI_MID

RING = 4
ZSRC = {}
for _j in range(JT):
    for _n, _o in (("hv", 0), ("hy", 512), ("hx", 1024), ("hg", 1536), ("rr", 2048), ("rk", 2560), ("rv", 3072),
                   ("rg", 3840), ("aq", 4352), ("ak", 4864), ("av", 5376), ("ag", 5888)):
        ZSRC[f"{_n}{_j}"] = _o + 128 * _j
ZSRC["wl"], ZSRC["al"] = 3584, 3712
for _b in range(3):
    for _j in range(KD):
        ZSRC[f"m{_b}{_j}"] = 6400 + 1024 * _b + 128 * _j
ORDER = [("filt",)] + [("ada", n, q) for n in range(6) for q in range(4)]
ORDER += [("z", f"{n}{j}") for j in range(JT) for n in ("hv", "hx")]
ORDER += [("z", f"{n}{j}") for j in range(JT) for n in ("hy", "hg")]
ORDER += [("z", f"{n}{j}") for j in range(JT) for n in ("aq", "ak")]
ORDER += [("z", f"av{j}") for j in range(JT)] + [("z", f"ag{j}") for j in range(JT)]
ORDER += [("lora",), ("z", "wl"), ("z", "al")]
ORDER += [("z", f"{n}{j}") for j in range(JT) for n in ("rk", "rr", "rv", "rg")]
for _p in range(KD // 2):
    for _b in range(3):
        ORDER += [("z", f"m{_b}{2 * _p}"), ("z", f"m{_b}{2 * _p + 1}"), ("br", _p, _b)]
ORDER += [("out", j) for j in range(KD)]
NSLOT = len(ORDER)
assert NSLOT % RING == 0
ZORDER = [k[1] for k in ORDER if k[0] == "z"]

PCOL, _at = {}, 0
for _n, _w in (("g", 8), ("bada", 24), ("cw0", 12), ("cw1", 12), ("cw2", 12), ("cb", 12), ("hyb", 4), ("mu", 14),
               ("w0", 8), ("a0", 8), ("kk", 4), ("ka", 4), ("rk", 4), ("lnw", 4), ("lnb", 4), ("gq", 1), ("gk", 1),
               ("gsub", 1), ("fb", 1), ("freq", 1), ("laminit", 1), ("oneml", 1),
               ("lq1", 64), ("lk1", 64), ("lq2", 64), ("lk2", 64)):
    PCOL[_n] = (_at, _w)
    _at += _w
NPAR = _at
CCOL, _at = {}, 0
LEVELS = [1, 2, 4, 8, 16, 32, 64]
for _n, _w in ([("ident", 128), ("ones", 128), ("bones", 128), ("rot", 128), ("cos", 512), ("sin", 512),
                ("feat", T), ("mfwd", 256), ("mbwd", 256), ("eps", 4), ("c", 16)]
               + [(f"lo{b}", 128) for b in LEVELS] + [(f"up{b}", 128) for b in LEVELS]):
    CCOL[_n] = (_at, _w)
    _at += _w
NCONST = _at
EPS_NORM, EPS_KK, EPS_GN, EPS_SUB = range(4)
DCOL, _at = {}, 0
for _n, _w in (("A", 16), ("B", 16), ("gate", 16), ("hmu", 14), ("ommu", 14), ("hw0", 8), ("ha0", 8), ("hka", 4),
               ("omka", 4), ("rkh", 4), ("gsl", 1), ("neglam", 1), ("ls", 4), ("mod", 48)):
    DCOL[_n] = (_at, _w)
    _at += _w
NDRV = _at
TABW = 2 * S
TABF = [(i * TABW, S) for i in range(4)] + [(4 * TABW, P)]


class Steps:

    def __init__(self, eng, sem):
        self.eng, self.sem, self.n = eng, sem, 0

    def next(self):
        self.n += 1
        return self.sem

    def settle(self):
        self.eng.wait_ge(self.sem, self.n)

    def again(self):
        self.n = 0


def build(nc, A):
    ctx = ExitStack()
    with ctx:
        def sb(name, cols, rows=128):
            return ctx.enter_context(nc.sbuf_tensor(name, [rows, cols], F32))

        per_layer = []

        def sem(name):
            return ctx.enter_context(nc.semaphore(name))

        def signal(name):
            per_layer.append(sem(name))
            return per_layer[-1]

        x = sb("x", KD * T)
        h = sb("h", KD * T)
        ya, yb, yc = sb("ya", JT * T), sb("yb", JT * T), sb("yc", JT * T)
        ring = sb("ring", RING * 1024)
        par = sb("par", NPAR)
        drv = sb("drv", NDRV)
        lora = sb("lora", 1024)
        cst = sb("cst", NCONST)
        resetm = ctx.enter_context(nc.sbuf_tensor("resetm", [128, T], mybir.dt.bfloat16))
        sc = sb("sc", 16)
        SCR = 24720
        scr = sb("scr", SCR)
        ps = ctx.enter_context(nc.psum_tensor("ps", [128, 4096], F32))

        def t3(ap, n):
            return ap.rearrange("p (a n) -> p a n", n=n)

        def xt(k):
            return x[:, k * T:(k + 1) * T]

        def ht(k):
            return h[:, k * T:(k + 1) * T]

        def tile(buf, j):
            return buf[:, j * T:(j + 1) * T]

        def pcol(name, i=0, n=1):
            o = PCOL[name][0] + i
            return par[:, o:o + n]

        def dcol(name, i=0, n=1):
            o = DCOL[name][0] + i
            return drv[:, o:o + n]

        def con(name):
            o, w = CCOL[name]
            return cst[:, o:o + w]

        def eps(i):
            return cst[:, CCOL["eps"][0] + i:CCOL["eps"][0] + i + 1]

        ident, ones, bones = con("ident"), con("ones"), con("bones")

        class Scratch:

            def __init__(self):
                self.at = 0

            def __call__(self, cols):
                a = scr[:, self.at:self.at + cols]
                self.at += cols
                assert self.at <= SCR, self.at
                return a

        sA = Scratch()
        p_in = sA(JT * T)
        u_v = [sA(T) for _ in range(2)]
        u_x = [sA(T) for _ in range(2)]
        hs = sA(NT * S)
        hd = sA(NT * S)
        tab = [sA(TABW) for _ in range(2)]
        yre = sA(NT * S)
        yim = sA(NT * S)
        Hre = [sA(S) for _ in range(2)]
        Him = [sA(S) for _ in range(2)]
        tA = [sA(T) for _ in range(4)]
        hid = sA(T)
        modrow = yre[:, 0:NT * S]
        modrow2 = yim[:, 0:NT * S]
        invt = scr[:, JT * T + 4 * T:JT * T + 4 * T + 4 * TABW + 2 * P]
        sB = Scratch()
        qb = [sB(HEADS * T) for _ in range(2)]
        kb = sB(HEADS * T)
        kP = sB(HEADS * P)
        vt = sB(NT * BR)
        vC = sB(BR)
        zc = [sB(T) for _ in range(2)]
        sq = [sB(T) for _ in range(2)]
        rr = [sB(T) for _ in range(2)]
        zn = [sB(T) for _ in range(2)]
        rope = [sB(S) for _ in range(2)]
        eb = [sB(2 * T) for _ in range(2)]
        pd = [sB(T) for _ in range(2)]
        pdT = sB(NT * S)
        stat = sB(16)
        gsb = yb
        sC = Scratch()
        tw, tal = sC(T), sC(T)
        r_, k_, v_, kkb, gs, kmix = (sC(T) for _ in range(6))
        vtok = sC(T)
        tC = [sC(T) for _ in range(6)]
        AR = sC(2 * T)
        Bt, Kt = sC(T), sC(T)
        Btok, Ktok = sC(T), sC(T)
        ABQ = [sC(2 * T) for _ in range(2)]
        AKQ = [sC(2 * T) for _ in range(2)]
        Aab = [sC(T) for _ in range(2)]
        Tm = [sC(T) for _ in range(2)]
        TT = [sC(T) for _ in range(2)]
        Ysb = Aab
        Xs = [sC(128) for _ in range(2)]
        Us = [sC(128) for _ in range(2)]
        Ms = [sC(64) for _ in range(2)]
        S0 = [sC(64) for _ in range(2)]
        Fin = [sC(64) for _ in range(2)]
        dec = sC(20)
        sD = Scratch()
        tg = [sD(T) for _ in range(2)]
        mg = sD(KD * T)
        tD = [sD(T) for _ in range(2)]

        def wide(b):
            return ps[:, 512 * b:512 * b + T]

        def ringslot(i):
            return ring[:, (i % RING) * 1024:(i % RING + 1) * 1024]

        w_full = [sem(f"w_full{i}") for i in range(RING)]
        w_used = sem("w_used")
        consts_in, x_in, x_ready = sem("consts_in"), sem("x_in"), sem("x_ready")
        y_stored, sc_tanh, sc_done = sem("y_stored"), sem("sc_tanh"), sem("sc_done")
        pre_step, begun = sem("pre_step"), sem("begun")
        par_in, win_in, inv_in, cache_in = (sem(n) for n in ("par_in", "win_in", "inv_in", "cache_in"))
        tab_in = [sem(f"tab_in{i}") for i in range(2)]
        TAB_LOADS = (3, 2)
        s0_in = [sem(f"s0_in{i}") for i in range(2)]
        kv_stored = sem("kv_stored")
        fin_stored = [sem(f"fin_stored{i}") for i in range(2)]
        tab_used = signal("tab_used")
        act_step, dve_step, layer_over = signal("act_step"), signal("dve_step"), signal("layer_over")
        act_phase, dve_phase = signal("act_phase"), signal("dve_phase")
        z_free = [signal(f"z_free{i}") for i in range(2)]
        hid_full, arg_ready, hid_ready = signal("hid_full"), signal("arg_ready"), signal("hid_ready")
        filt_full, filt_read = signal("filt_full"), signal("filt_read")
        mod_row, mod_cols, mod_done = signal("mod_row"), signal("mod_cols"), signal("mod_done")
        sq_ready, sq_used, rt_ready = signal("sq_ready"), signal("sq_used"), signal("rt_ready")
        xn_ready, h_ready = signal("xn_ready"), signal("h_ready")
        lin_ready, p_ready, pT_full, pT_ready = signal("lin_ready"), signal("p_ready"), signal("pT_full"), signal("pT_ready")
        H_full, H_ready, U_read, conv_full, conv_read = (signal(n) for n in ("H_full", "H_ready", "U_read", "conv_full", "conv_read"))
        tanh_ready = signal("tanh_ready")
        rot_full, qk_done, v_done, kP_ready, rms_full, rms_rt = (signal(n) for n in ("rot_full", "qk_done", "v_done", "kP_ready", "rms_full", "rms_rt"))
        q_zero = signal("q_zero")
        rms_sq, zn_ready = signal("rms_sq"), signal("zn_ready")
        s_full, s_max, e_ready, pd_ready, pT2_full, pT2_read, pv_full, o_ready = (signal(n) for n in (
            "s_full", "s_max", "e_ready", "pd_ready", "pT2_full", "pT2_read", "pv_full", "o_ready"))
        osq_ready, oss_full, ort_ready = signal("osq_ready"), signal("oss_full"), signal("ort_ready")
        lam_ready, lam_exp, onorm_done = signal("lam_ready"), signal("lam_exp"), signal("onorm_done")
        k_ready, kk_done, tw_lin, al_ready = (signal(n) for n in ("k_ready", "kk_done", "tw_lin", "al_ready"))
        lora_copied, tw_ready, kk_sq, kk_ss, kk_rt, v_ready = (signal(n) for n in (
            "lora_copied", "tw_ready", "kk_sq", "kk_ss", "kk_rt", "v_ready"))
        vT_full, vT_ready, la_full, th_ready, E_ready, ex_ready = (signal(n) for n in (
            "vT_full", "vT_ready", "la_full", "th_ready", "E_ready", "ex_ready"))
        BK_ready, BT_full, BT_ready, A_full, A_read, T_ready = (signal(n) for n in (
            "BK_ready", "BT_full", "BT_ready", "A_full", "A_read", "T_ready"))
        Y_full, Y_ready, D_full = signal("Y_full"), signal("Y_ready"), signal("D_full")
        X_full, X_ready, U2_full, U2_ready, M_full, M_ready, Yt_full, Yt_read = (signal(n) for n in (
            "X_full", "X_ready", "U2_full", "U2_ready", "M_full", "M_ready", "Yt_full", "Yt_read"))
        fin_ready, mu_full, mu_sub, gsq_ready, gss_full, grt_ready, bon_ready, bon_full = (signal(n) for n in (
            "fin_ready", "mu_full", "mu_sub", "gsq_ready", "gss_full", "grt_ready", "bon_ready", "bon_full"))
        br_full, br_read, merged_ready, out_read = (signal(n) for n in ("br_full", "br_read", "merged_ready", "out_read"))

        first, last = per_layer[0].num, per_layer[-1].num
        assert [p.num for p in per_layer] == list(range(first, last + 1))

        block = ctx.enter_context(nc.Block())

        @block.sync
        def _(sp):
            for s in range(RING):
                sp.dma_start(ringslot(s), A["w"][s, :, :]).then_inc(w_full[s], 16)
            with sp.Fori(0, DEPTH * NSLOT // RING - 1) as g:
                for s in range(RING):
                    sp.wait_ge(w_used, g * RING + (s + 1))
                    sp.dma_start(ringslot(s), A["w"][bass.ds(g * RING + (RING + s), 1), :, :].rearrange("a p n -> (a p) n")).then_inc(w_full[s], 16)

        @block.gpsimd
        def _(pool):
            pool.dma_start(cst[:, :], A["cst"][:, :]).then_inc(consts_in, 16)
            pool.dma_start(x[:, :], A["x"][:, :]).then_inc(x_in, 16)
            with pool.Fori(0, DEPTH) as l:
                pool.wait_ge(x_ready, l + 1)
                pool.sem_inc(begun, 1)

                def layer(a):
                    return a[bass.ds(l, 1), :, :].rearrange("a p n -> (a p) n")

                pool.dma_start(par[:, :], layer(A["par"])).then_inc(par_in, 16)
                pool.dma_start(yc[:, :], A["win"][:, :]).then_inc(win_in, 16)
                for f, (o, L) in enumerate(TABF):
                    if f >= 2:
                        pool.wait_ge(tab_used, f - 1)
                    pool.dma_start(tab[f % 2][:, 0:2 * L], A["tab"][:, o:o + 2 * L]).then_inc(tab_in[f % 2], 16)
                pool.wait_ge(tab_used, NT)
                pool.dma_start(invt, A["inv"][:, :]).then_inc(inv_in, 16)
                pool.wait_ge(dve_phase, 1)
                pool.wait_ge(act_phase, 1)
                pool.dma_start(t3(kb, T)[:, :, S:T], layer(A["ck"]).rearrange("p (a n) -> p a n", n=P)).then_inc(cache_in, 16)
                pool.dma_start(vC, layer(A["cv"])).then_inc(cache_in, 16)
                nc.gpsimd.memset(qb[0][64:128, :], 0.0).then_inc(q_zero, 1)
                nc.gpsimd.memset(qb[1][0:64, :], 0.0).then_inc(q_zero, 1)
                pool.wait_ge(kP_ready, HEADS)
                pool.dma_start(layer(A["new_k"]), kP).then_inc(kv_stored, 16)
                pool.wait_ge(v_done, JT)
                pool.dma_start(layer(A["new_v"]), t3(vt, BR)[:, NT - 1, :]).then_inc(kv_stored, 16)
                pool.wait_ge(kv_stored, l * 32 + 32)
                pool.sem_inc(begun, 1)
                pool.wait_ge(dve_phase, 2)
                pool.wait_ge(act_phase, 2)
                for g in range(2 * JT):
                    if g >= 2:
                        pool.wait_ge(fin_ready, g - 1)
                        pool.dma_start(A["new_s"][bass.ds(l, 1), :, (g - 2) * 64:(g - 1) * 64].rearrange("a p n -> (a p) n"),
                                       Fin[g % 2]).then_inc(fin_stored[g % 2], 16)
                    pool.dma_start(S0[g % 2], A["s0"][bass.ds(l, 1), :, g * 64:(g + 1) * 64].rearrange("a p n -> (a p) n")).then_inc(s0_in[g % 2], 16)
                for g in range(2 * JT, 2 * JT + 2):
                    pool.wait_ge(fin_ready, g - 1)
                    pool.dma_start(A["new_s"][bass.ds(l, 1), :, (g - 2) * 64:(g - 1) * 64].rearrange("a p n -> (a p) n"),
                                   Fin[g % 2]).then_inc(fin_stored[g % 2], 16)
                for b in range(2):
                    pool.wait_ge(fin_stored[b], l * (16 * JT) + 16 * JT)
                pool.sem_inc(layer_over, 1)
            pool.wait_ge(x_ready, DEPTH + 1)
            pool.dma_start(A["y"][:, :], x[:, :]).then_inc(y_stored, 16)
            pool.wait_ge(y_stored, 16)

        @block.tensor
        def _(pe):
            def mm(out, lhsT, rhs, start, stop):
                return nc.tensor.matmul(out, lhsT, rhs, start=start, stop=stop)

            def wide_mm(b, lhsT, rhs, start=True, stop=True, rows=None):
                o = wide(b) if rows is None else ps[rows, 512 * b:512 * b + T]
                mm(o[:, 0:S], lhsT, rhs[:, 0:S], start, stop)
                return mm(o[:, S:T], lhsT, rhs[:, S:T], start, stop)

            pe.wait_ge(consts_in, 16)
            pe.wait_ge(sc_done, 1)
            with pe.Fori(0, DEPTH) as l:
                pe.wait_ge(x_ready, l + 1)
                pe.sem_inc(begun, 1)

                def weights(*key):
                    i = ORDER.index(key)
                    pe.wait_ge(w_full[i % RING], l * (16 * NSLOT // RING) + 16 * (i // RING + 1))
                    return ringslot(i)

                def z_tile(name, tokens_first=False, first_marks=False):
                    n = ZORDER.index(name)
                    w = weights("z", name)
                    if n >= 2:
                        pe.wait_ge(z_free[n % 2], n // 2)
                    b = 2 * (n % 2)
                    if tokens_first:
                        for t in range(NT):
                            for k in range(KD):
                                i = mm(wide(b)[:, t * 128:(t + 1) * 128], ht(k)[:, t * 128:(t + 1) * 128],
                                       w[:, k * 128:(k + 1) * 128], k == 0, k == KD - 1)
                    else:
                        for k in range(KD):
                            for lo, hi in ((0, S), (S, T)):
                                i = mm(wide(b)[:, lo:hi], w[:, k * 128:(k + 1) * 128], ht(k)[:, lo:hi], k == 0, k == KD - 1)
                                if first_marks and k == 0 and lo == 0:
                                    i.then_inc(w_used, 1)
                    i.then_inc(w_used, 1)

                w = weights("filt",)
                pe.sem_inc(begun, 1)
                feat = con("feat")
                wide_mm(4, w[64:64 + HY_EMB, 64:128], feat[64:64 + HY_EMB, :], rows=slice(64, 128)).then_inc(hid_full, 1)
                pe.wait_ge(hid_ready, 1)
                wide_mm(6, w[64:128, 0:64], hid[64:128, :], rows=slice(0, 64)).then_inc(hid_full, 1)
                pe.wait_ge(hid_ready, 2)
                for t in range(NT):
                    b = 4 + 2 * (t % 2)
                    if t >= 2:
                        pe.wait_ge(filt_read, t - 1)
                    for s in range(2):
                        i = mm(ps[:, 512 * (b + s):512 * (b + s + 1)], hid[0:64, t * 128:(t + 1) * 128],
                               w[0:64, s * 512:(s + 1) * 512], True, True)
                    i.then_inc(filt_full, 1)
                for n in range(6):
                    if n >= 2:
                        pe.wait_ge(mod_row, n - 1)
                    for q in range(4):
                        w = weights("ada", n, q)
                        for kk in range(2):
                            k = 2 * q + kk
                            i = mm(ps[0:2, 1024 * (n % 2):1024 * (n % 2) + 512], sc[:, 2 * k:2 * k + 2], w[:, kk * 512:(kk + 1) * 512],
                                   k == 0, k == KD - 1)
                            if n == 0 and q == 0 and kk == 0:
                                i.then_inc(w_used, 1)
                        i.then_inc(w_used, 1)
                pe.wait_ge(mod_row, 6)
                for i_ in range(24):
                    row = (modrow if i_ < 16 else modrow2)[0:2, (i_ % 16) * 128:(i_ % 16) * 128 + 128]
                    i = nc.tensor.transpose(ps[:, 2 * i_:2 * i_ + 2], row, ident[0:2, 0:2])
                i.then_inc(mod_cols, 1)
                for k in range(KD):
                    pe.wait_ge(sq_ready, k + 1)
                    if k == 0:
                        pe.wait_ge(filt_read, NT)
                    i = wide_mm(4, ones, tA[k % 2], k == 0, k == KD - 1)
                    i.then_inc(sq_used, 1)
                for k in range(KD):
                    pe.wait_ge(h_ready, k + 1)

                def turn_p(j):
                    pe.wait_ge(p_ready, j + 1)
                    if j >= 2:
                        pe.wait_ge(pT_ready, j - 1)
                    if j == 0:
                        pe.wait_ge(rt_ready, 1)
                    b = 4 + 2 * (j % 2)
                    for t in range(NT):
                        i = nc.tensor.transpose(wide(b)[:, t * 128:(t + 1) * 128], tile(p_in, j)[:, t * 128:(t + 1) * 128], ident)
                    i.then_inc(pT_full, 1)

                for j in range(JT):
                    z_tile(f"hv{j}")
                    z_tile(f"hx{j}")
                    if j >= 1:
                        turn_p(j - 1)
                turn_p(JT - 1)
                pe.wait_ge(pT_ready, JT)
                for f, (o, L) in enumerate(TABF):
                    pe.wait_ge(tab_in[f % 2], l * (16 * TAB_LOADS[f % 2]) + 16 * (f // 2 + 1))
                    n = L // 128
                    t0 = 0 if f < 4 else NT - 1
                    w = tab[f % 2]
                    if f >= 1:
                        pe.wait_ge(H_ready, f)
                    for s, src in ((0, hs), (1, hd)):
                        for t in range(n):
                            i = mm(ps[:, 512 * (4 + s):512 * (5 + s)], w[:, s * L + t * 128:s * L + (t + 1) * 128],
                                   src[:, (t0 + t) * S:(t0 + t + 1) * S], t == 0, t == n - 1)
                    i.then_inc(H_full, 1)
                    if f >= 1:
                        pe.wait_ge(U_read, f)
                    for s in range(2):
                        for t in range(n):
                            i = mm(ps[:, 512 * (6 + s):512 * (7 + s)], w[:, s * L + t * 128:s * L + (t + 1) * 128],
                                   yb[:, (t0 + t) * S:(t0 + t + 1) * S], t == 0, t == n - 1)
                    i.then_inc(tab_used, 1)
                pe.wait_ge(inv_in, l * 16 + 16)
                for j in range(JT):
                    z_tile(f"hy{j}")
                    z_tile(f"hg{j}")
                    b = 4 + 2 * (j % 2)
                    if j == 0:
                        pe.wait_ge(U_read, NT)
                    if j >= 2:
                        pe.wait_ge(conv_read, j - 1)
                    for f in range(4):
                        for s, src in ((0, yre), (1, yim)):
                            mm(wide(b)[:, 0:S], src[:, f * S + j * 128:f * S + (j + 1) * 128],
                               invt[:, f * TABW + s * S:f * TABW + (s + 1) * S], f == 0 and s == 0, f == 3 and s == 1)
                    for s, src in ((0, yre), (1, yim)):
                        i = mm(wide(b)[:, S:T], src[:, 4 * S + j * 128:4 * S + (j + 1) * 128],
                               invt[:, 4 * TABW + s * P:4 * TABW + (s + 1) * P], s == 0, s == 1)
                    i.then_inc(conv_full, 1)

                def qk_norm(n):
                    pe.wait_ge(rms_sq, n + 1)
                    if n >= 1:
                        pe.wait_ge(rms_rt, n)
                    else:
                        pe.wait_ge(conv_read, JT)
                    wide_mm(4, bones, sq[n % 2]).then_inc(rms_full, 1)

                def qk_rotate(n):
                    pe.wait_ge(zn_ready, n + 1)
                    if n >= 2:
                        pe.wait_ge(qk_done, n - 1)
                    mm(ps[:, 512 * (6 + n % 2):512 * (7 + n % 2)], con("rot"), zn[n % 2][:, 0:S], True, True).then_inc(rot_full, 1)

                rest = [f"av{j}" for j in range(JT)] + [f"ag{j}" for j in range(JT)]
                for n in range(2 * JT):
                    z_tile(("aq", "ak")[n % 2] + str(n // 2))
                    if n >= 1:
                        qk_norm(n - 1)
                    if n >= 2:
                        qk_rotate(n - 2)
                for n, name in enumerate(rest):
                    z_tile(name, tokens_first=n < JT)
                    if n == 0:
                        qk_norm(2 * JT - 1)
                        qk_rotate(2 * JT - 2)
                    if n == 1:
                        qk_rotate(2 * JT - 1)
                nz = ZORDER.index("wl")
                for b in range(2):
                    pe.wait_ge(z_free[b], (nz - b + 1) // 2)
                pe.wait_ge(qk_done, 2 * JT)
                pe.wait_ge(cache_in, l * 32 + 32)
                pe.wait_ge(q_zero, 2)
                units = [(hd_, q) for hd_ in range(HEADS) for q in range(NT)]

                def scores(u):
                    hd_, q = units[u]
                    if u >= 2:
                        pe.wait_ge(e_ready, u - 1)
                    base = 1536 * (u % 2)
                    for m in range(2):
                        qq = tile(qb[m], hd_)[:, q * 128:(q + 1) * 128]
                        if q < 4:
                            kk = tile(kb, hd_)
                            cut = 512 - (m * T) % 512
                            mm(ps[:, base + m * T:base + m * T + cut], qq, kk[:, 0:cut], True, True)
                            i = mm(ps[:, base + m * T + cut:base + (m + 1) * T], qq, kk[:, cut:T], True, True)
                        else:
                            i = mm(ps[:, base + m * P:base + (m + 1) * P], qq, kP[:, hd_ * P:(hd_ + 1) * P], True, True)
                    i.then_inc(s_full, 1)

                def turn_pd(u):
                    hd_, q = units[u]
                    pe.wait_ge(pd_ready, u + 1)
                    if u >= 1:
                        pe.wait_ge(pT2_read, u)
                    if q == 0 and hd_ >= 1:
                        pe.wait_ge(o_ready, 2 * hd_)
                    for t in range(5 if q < 4 else 1):
                        i = nc.tensor.transpose(wide(6)[:, t * 128:(t + 1) * 128], pd[u % 2][:, t * 128:(t + 1) * 128], ident)
                    i.then_inc(pT2_full, 1)

                def weigh(hd_):
                    pe.wait_ge(pT2_read, NT * hd_ + 4)
                    if hd_ >= 1:
                        pe.wait_ge(o_ready, 2 * hd_ - 1)
                    for t in range(5):
                        vv = t3(vt, BR)[:, t, :] if t < 4 else vC
                        i = mm(ps[:, 3584:4096], vv[:, hd_ * 128:(hd_ + 1) * 128], pdT[:, t * S:(t + 1) * S], t == 0, t == 4)
                    i.then_inc(pv_full, 1)

                def weigh_ctx(hd_):
                    pe.wait_ge(pT2_read, NT * hd_ + 5)
                    mm(ps[:, 3200:3328], t3(vt, BR)[:, 4, hd_ * 128:(hd_ + 1) * 128], pctx,
                       True, True).then_inc(pv_full, 1)

                pctx = rope[0][:, 0:128]
                scores(0)
                scores(1)
                for u in range(len(units)):
                    if u + 2 < len(units):
                        scores(u + 2)
                    hd_, q = units[u]
                    turn_pd(u)
                    if q == 3:
                        weigh(hd_)
                    if q == 4:
                        weigh_ctx(hd_)
                for hd_ in range(HEADS):
                    pe.wait_ge(osq_ready, hd_ + 1)
                    if hd_ >= 2:
                        pe.wait_ge(ort_ready, hd_ - 1)
                    wide_mm(2 * (hd_ % 2), ones, sq[hd_ % 2]).then_inc(oss_full, 1)

                pe.wait_ge(dve_phase, 2)
                pe.wait_ge(act_phase, 2)
                pe.wait_ge(lora_copied, 1)
                z_tile("wl", first_marks=True)
                z_tile("al")
                for j in range(JT):
                    if j >= 1:
                        pe.wait_ge(bon_ready, 2 * j)
                    z_tile(f"rk{j}")
                    z_tile(f"rr{j}")
                    pe.wait_ge(kk_sq, j + 1)
                    wide_mm(4, bones, tC[0]).then_inc(kk_ss, 1)
                    z_tile(f"rv{j}")
                    z_tile(f"rg{j}")
                    pe.wait_ge(v_ready, j + 1)
                    for t in range(NT):
                        i = nc.tensor.transpose(wide(6)[:, t * 128:(t + 1) * 128], v_[:, t * 128:(t + 1) * 128], ident)
                    i.then_inc(vT_full, 1)
                    nzj = ZORDER.index(f"rg{j}") + 1
                    for d in range(2):
                        g = 2 * j + d
                        rows = slice(64 * d, 64 * d + 64)
                        if g == 0:
                            pe.wait_ge(tw_ready, 1)
                            pe.wait_ge(al_ready, 1)
                        if d == 0:
                            for b in range(2):
                                pe.wait_ge(z_free[b], (nzj - b + 1) // 2)
                            pe.wait_ge(kk_rt, j + 1)
                        else:
                            pe.wait_ge(Yt_read, g)
                            pe.wait_ge(fin_ready, g)
                        wide_mm(0, lora[rows, j * 128:(j + 1) * 128], tw[rows, :])
                        wide_mm(2, lora[rows, 512 + j * 128:512 + (j + 1) * 128], tal[rows, :]).then_inc(la_full, 1)
                        pe.wait_ge(BK_ready, g + 1)
                        if d == 0:
                            pe.wait_ge(vT_ready, j + 1)
                        for b, src in ((4, Bt), (6, Kt)):
                            for t in range(NT):
                                i = nc.tensor.transpose(wide(b)[:, t * 128:(t + 1) * 128], src[:, t * 128:(t + 1) * 128], ident)
                        i.then_inc(BT_full, 1)
                        for hh in range(2):
                            hr = slice(64 * hh, 64 * hh + 64)
                            for part in range(3):
                                n = 6 * g + 3 * hh + part
                                if hh == 0 and part == 1:
                                    pe.wait_ge(BT_ready, g + 1)
                                if hh == 1:
                                    pe.wait_ge(A_read, n - 2)
                                for c in range(NT):
                                    cc = slice(c * 128, (c + 1) * 128)
                                    if part < 2:
                                        o = 1536 * part + c * 256
                                        i = mm(ps[:, o:o + 256], (Bt, Kt)[part][hr, cc], AR[hr, c * 256:(c + 1) * 256], True, True)
                                    else:
                                        i = mm(wide(6)[:, cc], AR[hr, c * 256:c * 256 + 128], Bt[hr, cc], True, True)
                                i.then_inc(A_full, 1)
                        for lev in range(6):
                            n = 6 * g + lev
                            last_level = lev == 5
                            for hh in range(2):
                                pe.wait_ge(T_ready, 14 * g + 2 * lev + hh + 1)
                                if lev == 0 and hh == 0:
                                    pe.wait_ge(A_read, 6 * g + 6)
                                for c in range(NT):
                                    cc = slice(c * 128, (c + 1) * 128)
                                    i = mm(wide(4 * hh)[:, cc], ABQ[hh][:, c * 256:c * 256 + 128], Tm[hh][:, cc], True, True)
                                i.then_inc(Y_full, 1)
                            for part in (1,) if last_level else (0, 1):
                                for hh in range(2):
                                    if part == 0 or last_level:
                                        pe.wait_ge(Y_ready, 2 * n + hh + 1)
                                    for c in range(NT):
                                        cc = slice(c * 128, (c + 1) * 128)
                                        if part == 0:
                                            i = mm(wide(4 * hh + 2)[:, cc], TT[hh][:, cc], Ysb[hh][:, cc], True, True)
                                        else:
                                            i = mm(wide(4 * hh)[:, cc], Ysb[hh][:, cc], TT[hh][:, cc], True, True)
                                    i.then_inc(D_full, 1)
                        pe.wait_ge(T_ready, 14 * (g + 1))
                        order = [4] + ([0, 1, 2, 3] if d == 0 else [3, 2, 1, 0])
                        heads_of_tile = [(hh, slice(64 * hh, 64 * hh + 64)) for hh in range(2)]

                        def x_of_values(c, stop):
                            for hh, hr in heads_of_tile:
                                i = mm(ps[:, 512 * hh:512 * hh + 64], AKQ[hh][:, c * 256:c * 256 + 128],
                                       vtok[:, c * 128 + 64 * hh:c * 128 + 64 * hh + 64], True, stop)
                            return i

                        x_of_values(order[0], True).then_inc(X_full, 1)
                        for n, c in enumerate(order):
                            ns = 5 * g + n
                            cc = slice(c * 128, (c + 1) * 128)
                            M, Un = Ms[n % 2], Us[n % 2]
                            if n >= 1:
                                pe.wait_ge(M_ready, ns + 1)
                                for hh, hr in heads_of_tile:
                                    i = mm(ps[:, 512 * hh:512 * hh + 64], AR[hr, c * 256:c * 256 + 128], M[hr, :], False, True)
                                i.then_inc(X_full, 1)
                            for hh, hr in heads_of_tile:
                                tc_ = slice(c * 128 + 64 * hh, c * 128 + 64 * hh + 64)
                                mm(ps[hr, 1024:1088], Ktok[:, tc_], vtok[:, tc_], True, False)
                                if n:
                                    mm(ps[hr, 1024:1088], ident[hr, hr], M[hr, :], False, False)
                            pe.wait_ge(X_ready, ns + 1)
                            for hh, hr in heads_of_tile:
                                i = mm(ps[:, 1536 + 64 * hh:1536 + 64 * hh + 64], TT[hh][:, cc], Xs[n % 2][:, 64 * hh:64 * hh + 64], True, True)
                            i.then_inc(U2_full, 1)
                            if n < 4:
                                x_of_values(order[n + 1], False)
                            pe.wait_ge(U2_ready, ns + 1)
                            for hh, hr in heads_of_tile:
                                tc_ = slice(c * 128 + 64 * hh, c * 128 + 64 * hh + 64)
                                i = mm(ps[hr, 1024:1088], Btok[:, tc_], Un[:, 64 * hh:64 * hh + 64], False, True)
                            i.then_inc(M_full, 1)
                            for hh, hr in heads_of_tile:
                                tc_ = slice(c * 128 + 64 * hh, c * 128 + 64 * hh + 64)
                                o = ps[hr, 2048 + c * 128:2048 + (c + 1) * 128]
                                mm(o, vtok[:, tc_], AKQ[hh][:, c * 256 + 128:(c + 1) * 256], True, False)
                                if n:
                                    mm(o, M[hr, :], AR[hr, c * 256 + 128:(c + 1) * 256], False, False)
                                i = mm(o, Un[:, 64 * hh:64 * hh + 64], ABQ[hh][:, c * 256 + 128:(c + 1) * 256], False, True)
                        i.then_inc(Yt_full, 1)
                    pe.wait_ge(Yt_read, 2 * j + 2)
                    wide_mm(6, bones, tile(yb, j)).then_inc(mu_full, 1)
                    pe.wait_ge(gsq_ready, j + 1)
                    wide_mm(4, bones, tC[1]).then_inc(gss_full, 1)
                    pe.wait_ge(bon_ready, 2 * j + 1)
                    wide_mm(6, bones, tC[3]).then_inc(bon_full, 1)

                pe.wait_ge(bon_ready, 2 * JT)
                for p in range(KD // 2):
                    for b in range(3):
                        z_tile(f"m{b}{2 * p}")
                        z_tile(f"m{b}{2 * p + 1}")
                        w = weights("br", p, b)
                        for jj in range(2):
                            n = 6 * p + 2 * b + jj
                            if n >= 2:
                                pe.wait_ge(br_read, n - 1)
                            for k in range(JT):
                                i = wide_mm(4 + 2 * jj, w[:, (jj * JT + k) * 128:(jj * JT + k + 1) * 128], tile((ya, yb, yc)[b], k), k == 0, k == JT - 1)
                            i.then_inc(br_full if jj == 0 else w_used, 1)
                pe.wait_ge(merged_ready, KD)
                for j in range(KD):
                    w = weights("out", j)
                    if j >= 2:
                        pe.wait_ge(out_read, j - 1)
                    for k in range(KD):
                        i = wide_mm(4 + 2 * (j % 2), w[:, k * 128:(k + 1) * 128], tile(mg, k), k == 0, k == KD - 1)
                    i.then_inc(w_used, 1)
                pe.sem_inc(layer_over, 1)

        def used(key):
            return ORDER.index(key) + 1

        @block.scalar
        def _(act):
            step = Steps(act, act_step)
            A_ = nc.scalar.activation
            act.wait_ge(consts_in, 16)
            A_(sc[:, :], con("c"), ACT.Tanh, scale=0.5).then_inc(sc_tanh, 1)
            with act.Fori(0, DEPTH) as l:
                act.wait_ge(x_ready, l + 1)
                act.sem_inc(begun, 1)
                act.wait_ge(par_in, l * 16 + 16)

                def z_full(name):
                    act.wait_ge(w_used, l * NSLOT + used(("z", name)))
                    return wide(2 * (ZORDER.index(name) % 2))

                for n, rows in enumerate((slice(64, 128), slice(0, 64))):
                    act.wait_ge(arg_ready, n + 1)
                    A_(hid[rows, :], tA[0][rows, :], ACT.Sin).then_inc(hid_ready, 1)
                for n in range(6):
                    act.wait_ge(w_used, l * NSLOT + used(("ada", n, 3)))
                    dst = (modrow if n < 4 else modrow2)[0:2, (n % 4) * 512:(n % 4 + 1) * 512]
                    A_(dst, ps[0:2, 1024 * (n % 2):1024 * (n % 2) + 512], ACT.Copy).then_inc(mod_row, 1)
                act.wait_ge(filt_read, NT)
                for k in range(KD):
                    if k >= 2:
                        act.wait_ge(sq_used, k - 1)
                    A_(tA[k % 2], xt(k), ACT.Square).then_inc(sq_ready, 1)
                act.wait_ge(sq_used, KD)
                A_(hid[:, :], wide(4), ACT.Sqrt, scale=1.0 / D, bias=eps(EPS_NORM)).then_inc(rt_ready, 1)
                act.wait_ge(mod_done, 1)
                for k in range(KD):
                    act.wait_ge(xn_ready, k + 1)
                    for s, (lo, hi) in enumerate(((0, S), (S, T))):
                        i = A_(ht(k)[:, lo:hi], tA[2 + k % 2][:, lo:hi], ACT.Identity, scale=dcol("A", 2 * k + s), bias=dcol("B", 2 * k + s))
                        if s == 0:
                            i.then_inc(step.next(), 1)
                    i.then_inc(h_ready, 1)

                def lin(name, dst, w1, b):
                    z = z_full(name)
                    A_(dst, z, ACT.Identity, scale=w1, bias=b).then_inc(lin_ready, 1)

                def turned_p(j):
                    act.wait_ge(pT_full, j + 1)
                    A_(t3(yb[:, :], S)[:, :, j * 128:(j + 1) * 128], t3(wide(4 + 2 * (j % 2)), 128), ACT.Copy).then_inc(pT_ready, 1)

                for j in range(JT):
                    if j >= 2:
                        act.wait_ge(p_ready, j - 1)
                    lin(f"hv{j}", u_v[j % 2], pcol("cw1", j), pcol("cb", j))
                    lin(f"hx{j}", u_x[j % 2], pcol("cw1", 8 + j), pcol("cb", 8 + j))
                    if j >= 1:
                        turned_p(j - 1)
                turned_p(JT - 1)
                for f in range(NT):
                    act.wait_ge(H_full, f + 1)
                    if f >= 2:
                        act.wait_ge(U_read, f - 1)
                    A_(Hre[f % 2], ps[:, 2048:2560], ACT.Copy).then_inc(step.next(), 1)
                    A_(Him[f % 2], ps[:, 2560:3072], ACT.Copy).then_inc(H_ready, 1)
                for j in range(JT):
                    if j == 0:
                        act.wait_ge(p_ready, JT)
                    if j >= 2:
                        act.wait_ge(conv_read, j - 1)
                    lin(f"hy{j}", u_v[j % 2], pcol("cw1", 4 + j), pcol("cb", 4 + j))
                    A_(u_x[j % 2], z_full(f"hg{j}"), ACT.Tanh, scale=0.5).then_inc(tanh_ready, 1)
                act.wait_ge(tanh_ready, JT)
                act.sem_inc(act_phase, 1)
                act.wait_ge(dve_phase, 1)

                def qk_root(n):
                    act.wait_ge(rms_full, n + 1)
                    if n >= 2:
                        act.wait_ge(zn_ready, n - 1)
                    A_(rr[n % 2], wide(4), ACT.Sqrt, scale=1.0 / DH, bias=eps(EPS_NORM)).then_inc(rms_rt, 1)

                for n in range(2 * JT):
                    z = z_full(("aq", "ak")[n % 2] + str(n // 2))
                    if n >= 2:
                        act.wait_ge(zn_ready, n - 1)
                        act.wait_ge(rms_full, n - 1)
                    A_(zc[n % 2], z, ACT.Copy).then_inc(step.next(), 1)
                    A_(sq[n % 2], z, ACT.Square).then_inc(rms_sq, 1)
                    act.wait_ge(rms_sq, n + 1)
                    act.sem_inc(z_free[ZORDER.index(("aq", "ak")[n % 2] + str(n // 2)) % 2], 1)
                    if n >= 1:
                        qk_root(n - 1)
                qk_root(2 * JT - 1)
                for j in range(JT):
                    z = z_full(f"av{j}")
                    A_(t3(vt, BR)[:, :, j * 128:(j + 1) * 128], t3(z, 128), ACT.Copy).then_inc(v_done, 1)
                    act.wait_ge(v_done, j + 1)
                    act.sem_inc(z_free[ZORDER.index(f"av{j}") % 2], 1)
                for j in range(JT):
                    if j >= 2:
                        act.wait_ge(z_free[ZORDER.index(f"ag{j - 2}") % 2], ZORDER.index(f"ag{j - 2}") // 2 + 1)
                    if j == 0:
                        act.wait_ge(zn_ready, 2 * JT)
                    A_(zc[j % 2], z_full(f"ag{j}"), ACT.Tanh, scale=0.5).then_inc(tanh_ready, 1)
                units = [(hd_, q) for hd_ in range(HEADS) for q in range(NT)]
                pctx = rope[0][:, 0:128]

                def exps(u):
                    hd_, q = units[u]
                    act.wait_ge(s_max, u + 1)
                    if u >= 2:
                        act.wait_ge(pd_ready, u - 1)
                    w = T if q < 4 else P
                    for m in range(2):
                        st = stat[:, 8 * (u % 2):8 * (u % 2) + 8]
                        i = A_(eb[u % 2][:, m * T:m * T + w], ps[:, 1536 * (u % 2) + m * w:1536 * (u % 2) + (m + 1) * w], ACT.Exp,
                               scale=DH ** -0.5, bias=st[:, m:m + 1], accum_out=st[:, 2 + m:3 + m])
                        if m == 0:
                            i.then_inc(step.next(), 1)
                    i.then_inc(e_ready, 1)

                def turned_pd(u):
                    hd_, q = units[u]
                    act.wait_ge(pT2_full, u + 1)
                    if q == 0 and hd_ >= 1:
                        act.wait_ge(pv_full, 2 * hd_)
                    if q < 4:
                        A_(t3(pdT, S)[:, :, q * 128:(q + 1) * 128], t3(wide(6), 128), ACT.Copy).then_inc(pT2_read, 1)
                    else:
                        A_(pctx, ps[:, 3072:3200], ACT.Copy).then_inc(pT2_read, 1)

                def outputs(n):
                    hd_ = n // 2
                    act.wait_ge(pv_full, n + 1)
                    if n % 2 == 0:
                        A_(tile(yc, hd_)[:, 0:S], ps[:, 3584:4096], ACT.Copy).then_inc(o_ready, 1)
                    else:
                        A_(tile(yc, hd_)[:, S:T], ps[:, 3200:3328], ACT.Copy).then_inc(o_ready, 1)

                def head_root(n):
                    act.wait_ge(oss_full, n + 1)
                    if n >= 2:
                        act.wait_ge(onorm_done, n - 1)
                    A_(rr[n % 2], wide(2 * (n % 2)), ACT.Sqrt, scale=1.0 / (2 * DH), bias=eps(EPS_SUB)).then_inc(ort_ready, 1)

                act.wait_ge(lam_ready, 1)
                A_(dcol("ls", 2, 2), dcol("ls", 0, 2), ACT.Exp).then_inc(lam_exp, 1)
                for u in range(len(units)):
                    exps(u)
                    if u >= 1:
                        turned_pd(u - 1)
                        if units[u - 1][1] >= 3:
                            outputs(2 * units[u - 1][0] + units[u - 1][1] - 3)
                turned_pd(len(units) - 1)
                outputs(2 * HEADS - 1)
                act.wait_ge(o_ready, 2 * HEADS)
                for hd_ in range(HEADS):
                    if hd_ >= 2:
                        act.wait_ge(oss_full, hd_ - 1)
                    A_(sq[hd_ % 2], tile(yc, hd_), ACT.Square).then_inc(osq_ready, 1)
                    if hd_ >= 1:
                        head_root(hd_ - 1)
                head_root(HEADS - 1)
                act.wait_ge(ort_ready, HEADS)
                act.sem_inc(act_phase, 1)
                act.wait_ge(dve_phase, 2)

                i_l = ORDER.index(("lora",))
                act.wait_ge(w_full[i_l % RING], l * (16 * NSLOT // RING) + 16 * (i_l // RING + 1))
                A_(lora[:, :], ringslot(i_l), ACT.Copy).then_inc(lora_copied, 1)
                lin("wl", tw, dcol("ommu", 12), 0.0)
                lin("al", tal, dcol("ommu", 13), 0.0)
                act.wait_ge(tw_lin, 1)
                A_(tw, tw, ACT.Tanh).then_inc(tw_ready, 1)
                for j in range(JT):
                    if j >= 1:
                        act.wait_ge(bon_ready, 2 * j)
                    lin(f"rk{j}", k_, dcol("ommu", 4 + j), 0.0)
                    lin(f"rr{j}", r_, dcol("ommu", j), 0.0)
                    act.wait_ge(k_ready, j + 1)
                    A_(tC[0], k_, ACT.Square, scale=pcol("kk", j)).then_inc(kk_sq, 1)
                    act.wait_ge(kk_ss, j + 1)
                    A_(tC[1], wide(4), ACT.Sqrt, bias=eps(EPS_KK)).then_inc(kk_rt, 1)
                    lin(f"rv{j}", v_, dcol("ommu", 8 + j), 0.0)
                    A_(tC[2], z_full(f"rg{j}"), ACT.Tanh, scale=0.5).then_inc(tanh_ready, 1)
                    act.wait_ge(vT_full, j + 1)
                    A_(vtok, wide(6), ACT.Copy).then_inc(vT_ready, 1)
                    for d in range(2):
                        g = 2 * j + d
                        act.wait_ge(la_full, g + 1)
                        if d == 0:
                            act.wait_ge(kk_done, j + 1)
                        A_(tC[0], wide(0), ACT.Tanh, scale=0.5, bias=dcol("hw0", 4 * d + j)).then_inc(step.next(), 1)
                        A_(tC[5], wide(2), ACT.Tanh, scale=0.5, bias=dcol("ha0", 4 * d + j)).then_inc(th_ready, 1)
                        act.wait_ge(E_ready, g + 1)
                        E, Em = tC[2], tC[1]
                        A_(dec[:, 0:5], t3(E, 128)[:, :, 127], ACT.Exp, scale=KAPPA).then_inc(step.next(), 1)
                        A_(dec[:, 5:10], t3(Em, 128)[:, :, 0], ACT.Exp, scale=-KAPPA).then_inc(step.next(), 1)
                        for dst, (src, sg) in zip((tC[3], tC[4], tC[0]), (((E, 1), (Em, 1), (E, -1)), ((Em, -1), (E, -1), (Em, 1)))[d]):
                            A_(dst, src, ACT.Exp, scale=sg * KAPPA).then_inc(ex_ready, 1)
                        act.wait_ge(BT_full, g + 1)
                        A_(Btok, wide(4), ACT.Copy).then_inc(step.next(), 1)
                        A_(Ktok, wide(6), ACT.Copy).then_inc(BT_ready, 1)
                        for lev in range(6):
                            for hh in range(2):
                                n = 2 * (6 * g + lev) + hh
                                act.wait_ge(Y_full, n + 1)
                                A_(Ysb[hh], wide(4 * hh), ACT.Copy).then_inc(Y_ready, 1)
                        for n in range(5):
                            act.wait_ge(X_full, 5 * g + n + 1)
                            A_(t3(Xs[n % 2], 64), t3(ps[:, 0:1024], 512)[:, :, 0:64], ACT.Copy).then_inc(X_ready, 1)
                        if d == 0:
                            act.wait_ge(Yt_full, g + 1)
                            A_(tile(yb, j), wide(4), ACT.Copy).then_inc(Yt_read, 1)
                    act.wait_ge(mu_sub, j + 1)
                    A_(tC[1], tC[0], ACT.Square).then_inc(gsq_ready, 1)
                    act.wait_ge(gss_full, j + 1)
                    A_(tC[2], wide(4), ACT.Sqrt, scale=1.0 / 64, bias=eps(EPS_GN)).then_inc(grt_ready, 1)
                act.wait_ge(bon_ready, 2 * JT)
                for n in range(3 * KD):
                    p, b, jj = n // 6, n // 2 % 3, n % 2
                    name = f"m{b}{2 * p + jj}"
                    z = z_full(name)
                    if n >= 2:
                        act.wait_ge(br_read, n - 1)
                    A_(tg[n % 2], z, ACT.Tanh, scale=0.5).then_inc(tanh_ready, 1)
                    act.wait_ge(tanh_ready, 3 * JT + n + 1)
                    act.sem_inc(z_free[ZORDER.index(name) % 2], 1)
                act.sem_inc(layer_over, 1)

        @block.vector
        def _(dve):
            step = Steps(dve, pre_step)
            V = nc.vector
            STT, TTn, TS = V.scalar_tensor_tensor, V.tensor_tensor, V.tensor_scalar
            MUL, ADD, SUB = ALU.mult, ALU.add, ALU.subtract
            rs3 = resetm[:, :].rearrange("p (a n) -> p a n", n=128)
            V.memset(resetm[:, :], 1.0).then_inc(step.next(), 1)
            step.settle()
            V.memset(rs3[:, :, 0:1], 0.0).then_inc(step.next(), 1)
            dve.wait_ge(consts_in, 16)
            dve.wait_ge(sc_tanh, 1)
            STT(sc[:, :], sc[:, :], 1.0, con("c"), ADD, MUL).then_inc(step.next(), 1)
            step.settle()
            TS(sc[:, :], sc[:, :], 0.5, None, MUL).then_inc(sc_done, 1)
            dve.wait_ge(x_in, 16)
            dve.sem_inc(x_ready, 1)
            step = Steps(dve, dve_step)
            with dve.Fori(0, DEPTH) as l:
                step.again()
                dve.wait_ge(par_in, l * 16 + 16)

                def do(ins):
                    ins.then_inc(step.next(), 1)

                def link(ins):
                    ins.then_inc(step.next(), 1)
                    step.settle()

                do(TS(dcol("hmu", 0, 14), pcol("mu", 0, 14), 0.5, None, MUL))
                do(TS(dcol("ommu", 0, 14), pcol("mu", 0, 14), -1.0, 1.0, MUL, ADD))
                do(TS(dcol("hw0", 0, 8), pcol("w0", 0, 8), 0.5, None, MUL))
                do(TS(dcol("ha0", 0, 8), pcol("a0", 0, 8), 0.5, None, MUL))
                do(TS(dcol("hka", 0, 4), pcol("ka", 0, 4), 0.5, None, MUL))
                do(TS(dcol("omka", 0, 4), pcol("ka", 0, 4), -0.5, 1.0, MUL, ADD))
                do(TS(dcol("rkh", 0, 4), pcol("rk", 0, 4), 0.5, None, MUL))
                do(TTn(dcol("gsl"), pcol("gsub"), pcol("oneml"), MUL))
                do(TTn(pcol("lq1", 0, 64), pcol("lq1", 0, 64), pcol("lk1", 0, 64), MUL))
                link(TTn(pcol("lq2", 0, 64), pcol("lq2", 0, 64), pcol("lk2", 0, 64), MUL))
                do(V.tensor_reduce(dcol("ls", 0), pcol("lq1", 0, 64), AX.X, ADD))
                V.tensor_reduce(dcol("ls", 1), pcol("lq2", 0, 64), AX.X, ADD).then_inc(lam_ready, 1)

                for n, rows in enumerate((slice(64, 128), slice(0, 64))):
                    dve.wait_ge(hid_full, n + 1)
                    a, c = tA[1][rows, :], tA[2][rows, :]
                    fo, fr = PCOL["fb"][0], PCOL["freq"][0]
                    link(TS(a, ps[rows, 2048 + 1024 * n:2048 + 1024 * n + T], par[rows, fo:fo + 1], par[rows, fr:fr + 1], ADD, MUL))
                    link(TS(c, a, 1.0 / TWO_PI, ROUND, MUL, ADD))
                    link(TS(c, c, ROUND, None, SUB))
                    link(STT(a, c, -PI_HI, a, MUL, ADD))
                    link(STT(a, c, -PI_MID, a, MUL, ADD))
                    link(STT(a, c, -PI_LO, a, MUL, ADD))
                    TS(tA[0][rows, :], a, math.pi * (1 - 1e-7), -math.pi * (1 - 1e-7), ALU.min, ALU.max).then_inc(arg_ready, 1)
                dve.wait_ge(win_in, l * 16 + 16)
                for t in range(NT):
                    b = 2048 + 1024 * (t % 2)
                    dve.wait_ge(filt_full, t + 1)
                    hf, hb = tA[2 * (t % 2)][:, 0:S], tA[2 * (t % 2) + 1][:, 0:S]
                    win = yc[:, t * S:(t + 1) * S]
                    do(TTn(hf, ps[:, b:b + 512], win, MUL))
                    link(TTn(hb, ps[:, b + 512:b + 1024], win, MUL))
                    if t in (0, NT - 1):
                        link(V.memset(hb[0:1, :], 0.0))
                    do(TTn(hs[:, t * S:(t + 1) * S], hf, hb, ADD))
                    link(TTn(hd[:, t * S:(t + 1) * S], hb, hf, SUB))
                    dve.sem_inc(filt_read, 1)
                dve.wait_ge(mod_cols, 1)
                mod = dcol("mod", 0, 48)
                m3 = mod.rearrange("p (a n) -> p a n", n=2)
                link(TTn(m3, ps[:, 0:48].rearrange("p (a n) -> p a n", n=2), pcol("bada", 0, 24).unsqueeze(2).to_broadcast([128, 24, 2]), ADD))
                do(V.tensor_copy(dcol("B", 0, 16), mod[:, 0:16]))
                do(STT(dcol("A", 0, 16).rearrange("p (a n) -> p a n", n=2), m3[:, 8:16, :], 1.0, pcol("g", 0, 8).unsqueeze(2).to_broadcast([128, 8, 2]), ADD, MUL))
                link(TS(dcol("gate", 0, 16), mod[:, 32:48], 0.5, None, MUL))
                dve.sem_inc(mod_done, 1)
                dve.wait_ge(rt_ready, 1)
                rstd = tA[0]
                link(V.reciprocal(rstd, hid[:, :]))
                for k in range(KD):
                    if k >= 2:
                        dve.wait_ge(h_ready, k - 1)
                    TTn(tA[2 + k % 2], xt(k), rstd, MUL).then_inc(xn_ready, 1)

                n_lin = [0]

                def taps(name, u, w0, w2):
                    z = wide(2 * (ZORDER.index(name) % 2))
                    n_lin[0] += 1
                    dve.wait_ge(lin_ready, n_lin[0])
                    do(STT(u[:, 1:S], z[:, 0:S - 1], w0, u[:, 1:S], MUL, ADD))
                    link(STT(u[:, S + 1:T], z[:, S:T - 1], w0, u[:, S + 1:T], MUL, ADD))
                    do(STT(u[:, 0:S - 1], z[:, 1:S], w2, u[:, 0:S - 1], MUL, ADD))
                    link(STT(u[:, S:T - 1], z[:, S + 1:T], w2, u[:, S:T - 1], MUL, ADD))
                    dve.sem_inc(z_free[ZORDER.index(name) % 2], 1)

                n_tanh = [0]

                def silu_of(name, dst, th):
                    z = wide(2 * (ZORDER.index(name) % 2))
                    n_tanh[0] += 1
                    dve.wait_ge(tanh_ready, n_tanh[0])
                    link(STT(dst, th, 1.0, z, ADD, MUL))
                    dve.sem_inc(z_free[ZORDER.index(name) % 2], 1)

                for j in range(JT):
                    taps(f"hv{j}", u_v[j % 2], pcol("cw0", j), pcol("cw2", j))
                    taps(f"hx{j}", u_x[j % 2], pcol("cw0", 8 + j), pcol("cw2", 8 + j))
                    TTn(tile(p_in, j), u_v[j % 2], u_x[j % 2], MUL).then_inc(p_ready, 1)
                for f in range(NT):
                    dve.wait_ge(H_ready, f + 1)
                    dve.wait_ge(tab_used, f + 1)
                    Uc, Us_ = ps[:, 3072:3584], ps[:, 3584:4096]
                    o = slice(f * S, (f + 1) * S)
                    a, b, c, e = (t[:, 0:S] for t in tA)
                    do(TTn(a, Uc, Hre[f % 2], MUL))
                    do(TTn(b, Us_, Him[f % 2], MUL))
                    do(TTn(c, Us_, Hre[f % 2], MUL))
                    link(TTn(e, Uc, Him[f % 2], MUL))
                    do(TTn(yre[:, o], a, b, ADD))
                    link(TTn(yim[:, o], c, e, SUB))
                    dve.sem_inc(U_read, 1)
                for j in range(JT):
                    taps(f"hy{j}", u_v[j % 2], pcol("cw0", 4 + j), pcol("cw2", 4 + j))
                    gate = u_x[j % 2]
                    silu_of(f"hg{j}", gate, gate)
                    dve.wait_ge(conv_full, j + 1)
                    link(STT(tA[0], tile(p_in, j), pcol("hyb", j), wide(4 + 2 * (j % 2)), MUL, ADD))
                    link(TTn(tA[1], tA[0], u_v[j % 2], MUL))
                    link(STT(tile(ya, j), tA[1], 0.5, gate, MUL, MUL))
                    dve.sem_inc(conv_read, 1)
                dve.sem_inc(dve_phase, 1)
                dve.wait_ge(act_phase, 1)

                def normed(n):
                    dve.wait_ge(rms_rt, n + 1)
                    link(V.reciprocal(rr[n % 2], rr[n % 2]))
                    link(STT(zn[n % 2], zc[n % 2], pcol(("gq", "gk")[n % 2]), rr[n % 2], MUL, MUL))
                    dve.sem_inc(zn_ready, 1)

                def rotated(n):
                    j = n // 2
                    halves = (slice(0, 64), slice(64, 128))
                    if n % 2 == 0:
                        for m, rows in enumerate(halves):
                            do(V.tensor_copy(tile(qb[m], j)[rows, S:T], zn[n % 2][rows, S:T]))
                    else:
                        link(V.tensor_copy(kP[:, j * P:(j + 1) * P], zn[n % 2][:, S:T]))
                        dve.sem_inc(kP_ready, 1)
                    do(TTn(rope[0], zn[n % 2][:, 0:S], con("cos"), MUL))
                    dve.wait_ge(rot_full, n + 1)
                    link(TTn(rope[1], ps[:, 512 * (6 + n % 2):512 * (7 + n % 2)], con("sin"), MUL))
                    if n % 2 == 0:
                        for m, rows in enumerate(halves):
                            do(TTn(tile(qb[m], j)[rows, 0:S], rope[0][rows, :], rope[1][rows, :], ADD))
                        step.settle()
                    else:
                        link(TTn(tile(kb, j)[:, 0:S], rope[0], rope[1], ADD))
                    dve.sem_inc(qk_done, 1)

                for n in range(2 * JT):
                    normed(n)
                    if n >= 1:
                        rotated(n - 1)
                rotated(2 * JT - 1)
                for j in range(JT):
                    silu_of(f"ag{j}", tile(gsb, j), zc[j % 2])
                dve.wait_ge(lam_exp, 1)
                link(TTn(dcol("neglam"), dcol("ls", 3), dcol("ls", 2), SUB))
                link(TTn(dcol("neglam"), dcol("neglam"), pcol("laminit"), SUB))
                units = [(hd_, q) for hd_ in range(HEADS) for q in range(NT)]

                def maxima(u):
                    hd_, q = units[u]
                    w = T if q < 4 else P
                    st = stat[:, 8 * (u % 2):8 * (u % 2) + 8]
                    dve.wait_ge(s_full, u + 1)
                    link(V.tensor_reduce(st[:, 0:2], t3(ps[:, 1536 * (u % 2):1536 * (u % 2) + 2 * w], w), AX.X, ALU.max, negate=True))
                    TS(st[:, 0:2], st[:, 0:2], DH ** -0.5, None, MUL).then_inc(s_max, 1)

                def combine(u):
                    hd_, q = units[u]
                    w = T if q < 4 else P
                    st = stat[:, 8 * (u % 2):8 * (u % 2) + 8]
                    dve.wait_ge(e_ready, u + 1)
                    link(V.reciprocal(st[:, 4:6], st[:, 2:4]))
                    link(TTn(st[:, 6:7], st[:, 5:6], dcol("neglam"), MUL))
                    if u >= 2:
                        dve.wait_ge(pT2_full, u - 1)
                    link(TS(pd[u % 2][:, 0:w], eb[u % 2][:, T:T + w], st[:, 6:7], None, MUL))
                    link(STT(pd[u % 2][:, 0:w], eb[u % 2][:, 0:w], st[:, 4:5], pd[u % 2][:, 0:w], MUL, ADD))
                    dve.sem_inc(pd_ready, 1)

                maxima(0)
                for u in range(len(units)):
                    if u + 1 < len(units):
                        maxima(u + 1)
                    combine(u)
                for hd_ in range(HEADS):
                    dve.wait_ge(ort_ready, hd_ + 1)
                    link(V.reciprocal(rr[hd_ % 2], rr[hd_ % 2]))
                    link(STT(zn[0], tile(yc, hd_), dcol("gsl"), rr[hd_ % 2], MUL, MUL))
                    dve.sem_inc(onorm_done, 1)
                    link(STT(tile(yc, hd_), zn[0], 0.5, tile(gsb, hd_), MUL, MUL))
                dve.sem_inc(dve_phase, 1)
                dve.wait_ge(act_phase, 2)
                dve.wait_ge(kv_stored, l * 32 + 32)

                taps("wl", tw, dcol("hmu", 12), dcol("hmu", 12))
                dve.sem_inc(tw_lin, 1)
                taps("al", tal, dcol("hmu", 13), dcol("hmu", 13))
                dve.sem_inc(al_ready, 1)
                E, Em = tC[2], tC[1]

                def per_chunk(ap, i):
                    return t3(ap, 128)[:, :, i:i + 1].to_broadcast([128, NT, 128])

                def over_chunks(ap):
                    return ap.unsqueeze(1).to_broadcast([128, NT, ap.shape[1]])

                n_doubled = [0]
                for j in range(JT):
                    taps(f"rk{j}", k_, dcol("hmu", 4 + j), dcol("hmu", 4 + j))
                    dve.sem_inc(k_ready, 1)
                    taps(f"rr{j}", r_, dcol("hmu", j), dcol("hmu", j))
                    taps(f"rv{j}", v_, dcol("hmu", 8 + j), dcol("hmu", 8 + j))
                    dve.sem_inc(v_ready, 1)
                    dve.wait_ge(kk_rt, j + 1)
                    link(V.reciprocal(tC[1], tC[1]))
                    link(STT(kkb, k_, pcol("kk", j), tC[1], MUL, MUL))
                    silu_of(f"rg{j}", gs, tC[2])
                    dve.sem_inc(kk_done, 1)
                    for d in range(2):
                        g = 2 * j + d
                        dve.wait_ge(th_ready, g + 1)
                        u = tC[0]
                        link(TS(u, u, 1.0, None, ADD))
                        link(V.tensor_tensor_scan(tC[3], resetm[:, :], u, 0.0, MUL, ADD))
                        link(TTn(t3(E, 128), t3(tC[3], 128), per_chunk(tC[3], 63), SUB))
                        link(TTn(Em, E, u, SUB))
                        dve.sem_inc(E_ready, 1)
                        do(STT(Bt, tC[5], 1.0, kkb, ADD, MUL))
                        link(TS(tC[5], tC[5], dcol("hka", j), dcol("omka", j), MUL, ADD))
                        link(TTn(Kt, tC[5], k_, MUL))
                        if d == 0:
                            do(V.tensor_copy(kmix, Kt))
                        else:
                            do(TTn(kmix, kmix, Kt, ADD))
                        ar = AR.rearrange("p (a s n) -> p a s n", s=2, n=128)
                        dve.wait_ge(ex_ready, 3 * g + 1)
                        do(TTn(ar[:, :, 1, :], t3(r_, 128), t3(tC[3], 128), MUL))
                        dve.wait_ge(ex_ready, 3 * g + 2)
                        do(STT(ar[:, :, 0, :], t3(kkb, 128), -1.0, t3(tC[4], 128), MUL, MUL))
                        dve.wait_ge(ex_ready, 3 * g + 3)
                        step.settle()
                        do(STT(Bt, Bt, 0.5, tC[0], MUL, MUL))
                        link(TTn(Kt, Kt, tC[0], MUL))
                        dve.sem_inc(BK_ready, 1)
                        link(TTn(dec[:, 10:14], dec[:, 0:4], dec[:, 6:10], MUL))
                        msk = con(("mfwd", "mbwd")[d])
                        lo, up = ("lo", "up") if d == 0 else ("up", "lo")
                        for hh in range(2):
                            n = 6 * g + 3 * hh
                            dve.wait_ge(A_full, n + 1)
                            link(TTn(t3(ABQ[hh], 256), t3(ps[:, 0:2 * T], 256), over_chunks(msk), MUL))
                            dve.sem_inc(A_read, 1)
                            dve.wait_ge(A_full, n + 2)
                            link(TTn(t3(AKQ[hh], 256), t3(ps[:, 1536:1536 + 2 * T], 256), over_chunks(msk), MUL))
                            dve.sem_inc(A_read, 1)
                            dve.wait_ge(A_full, n + 3)
                            do(TTn(t3(Tm[hh], 128), t3(wide(6), 128), over_chunks(con(f"{lo}1")), MUL))
                            link(TTn(t3(TT[hh], 128), t3(ABQ[hh], 256)[:, :, 0:128], over_chunks(con(f"{up}1")), MUL))
                            dve.sem_inc(A_read, 1)
                            do(TTn(t3(Tm[hh], 128), t3(Tm[hh], 128), over_chunks(ident), ADD))
                            link(TTn(t3(TT[hh], 128), t3(TT[hh], 128), over_chunks(ident), ADD))
                            dve.sem_inc(T_ready, 1)
                        for lev in range(6):
                            for part in (0, 1) if lev < 5 else (1,):
                                for hh in range(2):
                                    n_doubled[0] += 1
                                    dve.wait_ge(D_full, n_doubled[0])
                                    m = con(f"{(lo, up)[part]}{LEVELS[lev + 1]}").bitcast(I32)
                                    link(V.copy_predicated(t3((Tm, TT)[part][hh], 128), over_chunks(m), t3(wide(4 * hh + 2 - 2 * part), 128)))
                                    if part == 1:
                                        dve.sem_inc(T_ready, 1)
                        dve.wait_ge(s0_in[g % 2], l * (16 * JT) + 16 * (g // 2 + 1))
                        order = [4] + ([0, 1, 2, 3] if d == 0 else [3, 2, 1, 0])
                        dve.sem_inc(M_ready, 1)
                        for n, c in enumerate(order):
                            ns = 5 * g + n
                            dve.wait_ge(U2_full, ns + 1)
                            V.tensor_copy(Us[n % 2], ps[:, 1536:1664]).then_inc(U2_ready, 1)
                            dve.wait_ge(M_full, ns + 1)
                            if n == 0:
                                if g >= 2:
                                    dve.wait_ge(fin_stored[g % 2], l * (16 * JT) + 16 * (g // 2))
                                do(TS(Fin[g % 2], ps[:, 1024:1088], dec[:, 4 + 5 * d:5 + 5 * d], None, MUL))
                                o = 5 if d == 0 else 3
                                link(TS(Ms[1], S0[g % 2], dec[:, o:o + 1], None, MUL))
                                dve.sem_inc(M_ready, 1)
                            elif n < 4:
                                o = 10 + (c if d == 0 else c - 1)
                                link(TS(Ms[(n + 1) % 2], ps[:, 1024:1088], dec[:, o:o + 1], None, MUL))
                                dve.sem_inc(M_ready, 1)
                        dve.sem_inc(fin_ready, 1)
                        if d == 1:
                            dve.wait_ge(Yt_full, g + 1)
                            link(TTn(tile(yb, j), tile(yb, j), wide(4), ADD))
                            dve.sem_inc(Yt_read, 1)
                    dve.wait_ge(mu_full, j + 1)
                    link(STT(tC[0], wide(6), -1.0 / 64, tile(yb, j), MUL, ADD))
                    dve.sem_inc(mu_sub, 1)
                    link(STT(tC[3], r_, dcol("rkh", j), kmix, MUL, MUL))
                    dve.sem_inc(bon_ready, 1)
                    dve.wait_ge(grt_ready, j + 1)
                    link(V.reciprocal(tC[2], tC[2]))
                    link(STT(tC[4], tC[0], pcol("lnw", j), tC[2], MUL, MUL))
                    dve.wait_ge(bon_full, j + 1)
                    link(TTn(tC[5], wide(6), v_, MUL))
                    link(STT(tC[4], tC[4], pcol("lnb", j), tC[5], ADD, ADD))
                    link(STT(tile(yb, j), tC[4], 0.5, gs, MUL, MUL))
                    dve.sem_inc(bon_ready, 1)

                for n in range(3 * KD):
                    p, b, jj = n // 6, n // 2 % 3, n % 2
                    dve.wait_ge(tanh_ready, 3 * JT + n + 1)
                    if jj == 0:
                        dve.wait_ge(br_full, n // 2 + 1)
                    else:
                        dve.wait_ge(w_used, l * NSLOT + used(("br", p, b)))
                    dst = tile(mg, 2 * p + jj)
                    link(STT(dst if b == 0 else tD[jj], tg[n % 2], 1.0, wide(4 + 2 * jj), ADD, MUL))
                    dve.sem_inc(br_read, 1)
                    if b:
                        link(TTn(dst, dst, tD[jj], ADD))
                    if b == 2:
                        dve.sem_inc(merged_ready, 1)
                for j in range(KD):
                    dve.wait_ge(w_used, l * NSLOT + used(("out", j)))
                    z = wide(4 + 2 * (j % 2))
                    for s, (lo_, hi_) in enumerate(((0, S), (S, T))):
                        do(STT(xt(j)[:, lo_:hi_], z[:, lo_:hi_], dcol("gate", 2 * j + s), xt(j)[:, lo_:hi_], MUL, ADD))
                    step.settle()
                    dve.sem_inc(out_read, 1)
                dve.wait_ge(layer_over, 3)
                dve.sem_clear(range(first, last + 1))
                dve.sem_inc(x_ready, 1)


def _tables():
    c = np.zeros((128, NCONST), np.float32)

    def put(name, a, row=0):
        o, w = CCOL[name]
        c[row:row + a.shape[0], o:o + a.shape[1]] = a

    i = np.arange(128)
    put("ident", np.eye(128))
    put("ones", np.ones((128, 128)))
    put("bones", (i[:, None] // 64 == i[None, :] // 64).astype(np.float32))
    rot = np.zeros((128, 128))
    for m in range(128):
        if m % 32 < 16:
            rot[m + 16, m] = -1.0
        else:
            rot[m - 16, m] = 1.0
    put("rot", rot)
    freqs = (10000.0 ** (-np.arange(16, dtype=np.float32) / np.float32(16))).astype(np.float32)
    t = np.arange(S)
    pos = np.where((i % 64)[:, None] < 32, (t // GRID_W)[None, :], (t % GRID_W)[None, :]).astype(np.float32)
    ang = (pos * freqs[i % 16][:, None]).astype(np.float64)
    put("cos", np.cos(ang))
    put("sin", np.sin(ang))
    feats, wins = [], []
    deltas = np.abs(np.linspace(math.log(1e-2) / 1.5, math.log(1e-2) / 0.3, BR))
    bands = np.linspace(1e-4, 15, 16)[:, None]
    for L in (S, P):
        tl = np.linspace(0.0, 1.0, L)
        w = 2.0 * math.pi * np.arange(L)[None, :] / L
        feats.append(np.concatenate([tl[None, :], np.cos(bands * w), -np.sin(bands * w)], 0))
        wins.append(np.exp(-tl[:, None] * deltas[None, :]))
    put("feat", np.concatenate(feats, 1), 64)
    up, upi = (i[:, None] < i[None, :]), (i[:, None] <= i[None, :])
    put("mfwd", np.concatenate([up, upi], 1))
    put("mbwd", np.concatenate([up.T, upi.T], 1))
    put("eps", np.tile([[1e-6, 1e-12, 64e-5, 1e-5]], (128, 1)))
    for b in LEVELS:
        lo = ((i[:, None] // b) % 2 == 1) & (i[None, :] // b == i[:, None] // b - 1)
        put(f"lo{b}", lo)
        put(f"up{b}", lo.T)
    win = np.concatenate(wins, 0).reshape(NT, 128, BR).transpose(1, 0, 2).reshape(128, NT * BR)
    tab, inv = [], []
    for L in (S, P):
        om = 2.0 * math.pi * (np.arange(L) + 0.5) / (2 * L)
        a = np.arange(L)[:, None] * om[None, :]
        for f in range(L // 128):
            for fn in (np.cos, np.sin):
                tab.append(fn(a[:, f * 128:(f + 1) * 128]).reshape(L // 128, 128, 128).transpose(1, 0, 2).reshape(128, L))
                inv.append(fn(a[:, f * 128:(f + 1) * 128]).T / L)
    f32 = np.float32
    return c, win.astype(f32), np.concatenate(tab, 1).astype(f32), np.concatenate(inv, 1).astype(f32)


def _pack(v):
    f32 = np.float32
    cst, win, tab, inv = _tables()
    o = CCOL["c"][0]
    cst[:, o:o + 16:2] = v["c"].reshape(KD, 128).T
    cst[:, o + 1:o + 16:2] = v["c_ctx"].reshape(KD, 128).T
    w = np.zeros((DEPTH, NSLOT, 128, 1024), f32)
    par = np.zeros((DEPTH, 128, NPAR), f32)
    for l in range(DEPTH):
        def col_tile(m, o):
            return m[:, o:o + 128].reshape(-1, 128, 128).transpose(1, 0, 2).reshape(128, -1)

        for i, key in enumerate(ORDER):
            if key[0] == "z":
                w[l, i] = col_tile(v["w_in"][l], ZSRC[key[1]])
            elif key[0] == "out":
                w[l, i] = col_tile(v["w_out"][l], 128 * key[1])
            elif key[0] == "br":
                w[l, i] = np.concatenate([col_tile(v["w_br"][l, key[2]], 128 * (2 * key[1] + jj)) for jj in range(2)], 1)
            elif key[0] == "ada":
                a = v["w_ada"][l][256 * key[2]:256 * (key[2] + 1), 512 * key[1]:512 * (key[1] + 1)]
                w[l, i] = a.reshape(2, 128, 512).transpose(1, 0, 2).reshape(128, 1024)
            elif key[0] == "filt":
                w[l, i, 0:64] = v["hy_f3"][l]
                w[l, i, 64:128, 0:64] = v["hy_f2"][l]
                w[l, i, 64:64 + HY_EMB, 64:128] = v["hy_f1"][l]
            else:
                w[l, i, :, 0:512] = v["rw_w2"][l].reshape(128, 512)
                w[l, i, :, 512:1024] = v["rw_a2"][l].reshape(128, 512)

        def put(name, a):
            o, n = PCOL[name]
            par[l, :, o:o + n] = a

        def cols(a):
            return np.asarray(a).reshape(-1, 128).T

        put("g", cols(v["norm_g"][l]))
        put("bada", cols(v["b_ada"][l]))
        for n in range(3):
            put(f"cw{n}", cols(v["hy_conv_w"][l, n]))
        put("cb", cols(v["hy_conv_b"][l]))
        put("hyb", cols(v["hy_bias"][l]))
        for name, key in (("mu", "rw_mu"), ("w0", "rw_w0"), ("a0", "rw_a0"), ("kk", "rw_kk"), ("ka", "rw_ka"),
                          ("rk", "rw_rk"), ("lnw", "rw_ln_w"), ("lnb", "rw_ln_b"), ("gsub", "da_gsub")):
            put(name, cols(v[key][l]))
        put("gq", np.tile(v["da_gq"][l], 2)[:, None])
        put("gk", np.tile(v["da_gk"][l], 2)[:, None])
        put("fb", np.concatenate([v["hy_fb2"][l], v["hy_fb1"][l]])[:, None])
        put("freq", np.tile(v["hy_freq"][l], 2)[:, None])
        lam = 0.8 - 0.6 * math.exp(-0.3 * l)
        put("laminit", np.full((128, 1), lam, f32))
        put("oneml", np.full((128, 1), 1.0 - lam, f32))
        for name in ("lq1", "lk1", "lq2", "lk2"):
            put(name, np.broadcast_to(v[f"da_{name}"][l], (128, 64)))
    xt = np.concatenate([v["x_sample"][0], v["x_prompt"][0]], 0).T
    s0 = v["state_rwkv"][0].reshape(DEPTH, 2, JT, 2, 64, 64).transpose(0, 3, 5, 2, 1, 4)
    return {
        "w": w.reshape(DEPTH * NSLOT, 128, 1024), "par": par, "cst": cst, "win": win, "tab": tab, "inv": inv,
        "x": xt.reshape(KD, 128, T).transpose(1, 0, 2).reshape(128, KD * T),
        "ck": v["cache_k"][0].transpose(0, 3, 4, 2, 1).reshape(DEPTH, 128, HEADS * PAST),
        "cv": v["cache_v"][0].reshape(DEPTH, PAST, BR),
        "s0": s0.reshape(DEPTH, 128, 512),
    }


def kernel(**inputs):
    import numpy as _np
    import concourse.bacc as _bacc
    from concourse.bass_utils import run_bass_kernel_spmd as _run

    arrays = {k: _np.ascontiguousarray(a) for k, a in _pack({k: _np.asarray(a) for k, a in inputs.items()}).items()}
    outs = {"y": (128, KD * T), "new_k": (DEPTH, 128, HEADS * P), "new_v": (DEPTH, P, BR), "new_s": (DEPTH, 128, 512)}
    nc = _bacc.Bacc("TRN2", target_bir_lowering=False, num_devices=1)
    args = {k: nc.dram_tensor(f"in_{k}", a.shape, F32, kind="ExternalInput").ap() for k, a in arrays.items()}
    args.update({k: nc.dram_tensor(f"out_{k}", s, F32, kind="ExternalOutput").ap() for k, s in outs.items()})
    build(nc, args)
    r = _run(nc, [{f"in_{k}": a for k, a in arrays.items()}], core_ids=[0]).results[0]
    y = _np.asarray(r["out_y"]).reshape(128, KD, T).transpose(2, 1, 0).reshape(T, D)
    new_k = _np.asarray(r["out_new_k"]).reshape(DEPTH, 2, DH, HEADS, P).transpose(0, 4, 3, 1, 2)[None]
    new_v = _np.asarray(r["out_new_v"]).reshape(DEPTH, P, HEADS, 2 * DH)[None]
    new_s = _np.asarray(r["out_new_s"]).reshape(DEPTH, 2, 64, JT, 2, 64).transpose(0, 4, 3, 1, 5, 2).reshape(1, DEPTH, 2, 8, 64, 64)
    c = _np.ascontiguousarray
    return c(y[None, S:T]), c(y[None, 0:S]), c(new_k), c(new_v), c(new_s)
```

```python
import math
from contextlib import ExitStack

import numpy as np
import concourse.bass as bass
from concourse import mybir

F32 = mybir.dt.float32
I32 = mybir.dt.int32
ALU = mybir.AluOpType
ACT = mybir.ActivationFunctionType
AX = mybir.AxisListType

DEPTH, D, S, P, PAST = 2, 1024, 512, 128, 128
T = S + P
KD = D // 128
BR = 512
JT = BR // 128
NT = T // 128
HEADS = 4
DH = 64
GRID_W = 64
HY_EMB = 33
DECAY = math.exp(-0.5)
KAPPA = -0.5 * DECAY
TWO_PI = 2.0 * math.pi
ROUND = 12582912.0
PI_HI, PI_MID = 6.28125, 0.0019350051879882812
PI_LO = TWO_PI - PI_HI - PI_MID

RING = 4
ZSRC = {}
for _j in range(JT):
    for _n, _o in (("hv", 0), ("hy", 512), ("hx", 1024), ("hg", 1536), ("rr", 2048), ("rk", 2560), ("rv", 3072),
                   ("rg", 3840), ("aq", 4352), ("ak", 4864), ("av", 5376), ("ag", 5888)):
        ZSRC[f"{_n}{_j}"] = _o + 128 * _j
ZSRC["wl"], ZSRC["al"] = 3584, 3712
for _b in range(3):
    for _j in range(KD):
        ZSRC[f"m{_b}{_j}"] = 6400 + 1024 * _b + 128 * _j
ORDER = [("filt",)] + [("ada", n, q) for n in range(6) for q in range(4)]
ORDER += [("z", f"{n}{j}") for j in range(JT) for n in ("hv", "hx")]
ORDER += [("z", f"{n}{j}") for j in range(JT) for n in ("hy", "hg")]
ORDER += [("z", f"{n}{j}") for j in range(JT) for n in ("aq", "ak")]
ORDER += [("z", f"av{j}") for j in range(JT)] + [("z", f"ag{j}") for j in range(JT)]
ORDER += [("lora",), ("z", "wl"), ("z", "al")]
ORDER += [("z", f"{n}{j}") for j in range(JT) for n in ("rk", "rr", "rv", "rg")]
for _p in range(KD // 2):
    for _b in range(3):
        ORDER += [("z", f"m{_b}{2 * _p}"), ("z", f"m{_b}{2 * _p + 1}"), ("br", _p, _b)]
ORDER += [("out", j) for j in range(KD)]
NSLOT = len(ORDER)
assert NSLOT % RING == 0
ZORDER = [k[1] for k in ORDER if k[0] == "z"]

PCOL, _at = {}, 0
for _n, _w in (("g", 8), ("bada", 24), ("cw0", 12), ("cw1", 12), ("cw2", 12), ("cb", 12), ("hyb", 4), ("mu", 14),
               ("w0", 8), ("a0", 8), ("kk", 4), ("ka", 4), ("rk", 4), ("lnw", 4), ("lnb", 4), ("gq", 1), ("gk", 1),
               ("gsub", 1), ("fb", 1), ("freq", 1), ("laminit", 1), ("oneml", 1),
               ("lq1", 64), ("lk1", 64), ("lq2", 64), ("lk2", 64)):
    PCOL[_n] = (_at, _w)
    _at += _w
NPAR = _at
CCOL, _at = {}, 0
LEVELS = [1, 2, 4, 8, 16, 32, 64]
for _n, _w in ([("ident", 128), ("ones", 128), ("bones", 128), ("rot", 128), ("cos", 512), ("sin", 512),
                ("feat", T), ("mfwd", 256), ("mbwd", 256), ("eps", 4), ("c", 16)]
               + [(f"lo{b}", 128) for b in LEVELS] + [(f"up{b}", 128) for b in LEVELS]):
    CCOL[_n] = (_at, _w)
    _at += _w
NCONST = _at
EPS_NORM, EPS_KK, EPS_GN, EPS_SUB = range(4)
DCOL, _at = {}, 0
for _n, _w in (("A", 16), ("B", 16), ("gate", 16), ("hmu", 14), ("ommu", 14), ("hw0", 8), ("ha0", 8), ("hka", 4),
               ("omka", 4), ("rkh", 4), ("gsl", 1), ("neglam", 1), ("ls", 4), ("gq8", 1), ("mod", 48)):
    DCOL[_n] = (_at, _w)
    _at += _w
NDRV = _at
TABW = 2 * S
TABF = [(i * TABW, S) for i in range(4)] + [(4 * TABW, P)]


class Steps:

    def __init__(self, eng, sem):
        self.eng, self.sem, self.n = eng, sem, 0

    def next(self):
        self.n += 1
        return self.sem

    def settle(self):
        self.eng.wait_ge(self.sem, self.n)

    def again(self):
        self.n = 0


def build(nc, A):
    ctx = ExitStack()
    with ctx:
        def sb(name, cols, rows=128):
            return ctx.enter_context(nc.sbuf_tensor(name, [rows, cols], F32))

        per_layer = []

        def sem(name):
            return ctx.enter_context(nc.semaphore(name))

        def signal(name):
            per_layer.append(sem(name))
            return per_layer[-1]

        x = sb("x", KD * T)
        h = sb("h", KD * T)
        ya, yb, yc = sb("ya", JT * T), sb("yb", JT * T), sb("yc", JT * T)
        ring = sb("ring", RING * 1024)
        par = sb("par", NPAR)
        drv = sb("drv", NDRV)
        lora = sb("lora", 1024)
        cst = sb("cst", NCONST)
        resetm = ctx.enter_context(nc.sbuf_tensor("resetm", [128, T], mybir.dt.bfloat16))
        sc = sb("sc", 16)
        SCR = 24720
        scr = sb("scr", SCR)
        ps = ctx.enter_context(nc.psum_tensor("ps", [128, 4096], F32))

        def t3(ap, n):
            return ap.rearrange("p (a n) -> p a n", n=n)

        def xt(k):
            return x[:, k * T:(k + 1) * T]

        def ht(k):
            return h[:, k * T:(k + 1) * T]

        def tile(buf, j):
            return buf[:, j * T:(j + 1) * T]

        def pcol(name, i=0, n=1):
            o = PCOL[name][0] + i
            return par[:, o:o + n]

        def dcol(name, i=0, n=1):
            o = DCOL[name][0] + i
            return drv[:, o:o + n]

        def con(name):
            o, w = CCOL[name]
            return cst[:, o:o + w]

        def eps(i):
            return cst[:, CCOL["eps"][0] + i:CCOL["eps"][0] + i + 1]

        ident, ones, bones = con("ident"), con("ones"), con("bones")

        class Scratch:

            def __init__(self):
                self.at = 0

            def __call__(self, cols):
                a = scr[:, self.at:self.at + cols]
                self.at += cols
                assert self.at <= SCR, self.at
                return a

        sA = Scratch()
        p_in = sA(JT * T)
        u_v = [sA(T) for _ in range(2)]
        u_x = [sA(T) for _ in range(2)]
        hs = sA(NT * S)
        hd = sA(NT * S)
        tab = [sA(TABW) for _ in range(2)]
        yre = sA(NT * S)
        yim = sA(NT * S)
        Hre = [sA(S) for _ in range(2)]
        Him = [sA(S) for _ in range(2)]
        tA = [sA(T) for _ in range(4)]
        hid = sA(T)
        modrow = yre[:, 0:NT * S]
        modrow2 = yim[:, 0:NT * S]
        invt = scr[:, JT * T + 4 * T:JT * T + 4 * T + 4 * TABW + 2 * P]
        sB = Scratch()
        qb = [sB(HEADS * T) for _ in range(2)]
        kb = sB(HEADS * T)
        kP = sB(HEADS * P)
        vt = sB(NT * BR)
        vC = sB(BR)
        zc = [sB(T) for _ in range(2)]
        sq = [sB(T) for _ in range(2)]
        rr = [sB(T) for _ in range(2)]
        zn = [sB(T) for _ in range(2)]
        rope = [sB(S) for _ in range(2)]
        eb = [sB(2 * T) for _ in range(2)]
        pd = [sB(T) for _ in range(2)]
        pdT = sB(NT * S)
        stat = sB(16)
        gsb = yb
        sC = Scratch()
        tw, tal = sC(T), sC(T)
        r_, k_, v_, kkb, gs, kmix = (sC(T) for _ in range(6))
        vtok = sC(T)
        tC = [sC(T) for _ in range(6)]
        merge_at = sC.at
        AR = sC(2 * T)
        Bt, Kt = sC(T), sC(T)
        Btok, Ktok = sC(T), sC(T)
        ABQ = [sC(2 * T) for _ in range(2)]
        AKQ = [sC(2 * T) for _ in range(2)]
        Tm = [sC(T) for _ in range(2)]
        TT = [sC(T) for _ in range(2)]
        Ysb = [sC(T) for _ in range(2)]
        Xs = [sC(128) for _ in range(2)]
        Us = [sC(128) for _ in range(2)]
        Ms = [sC(64) for _ in range(2)]
        S0 = [sC(64) for _ in range(2)]
        Fin = [sC(64) for _ in range(2)]
        th1 = [sC(T) for _ in range(2)]
        dec = [sC(20) for _ in range(2)]
        kksq, kkrt, gth = AKQ[1][:, 0:T], AKQ[1][:, T:2 * T], AKQ[0][:, 0:T]
        sD = Scratch()
        sD.at = merge_at
        tg = [sD(T) for _ in range(2)]
        mg = sD(KD * T)
        tD = [sD(T) for _ in range(2)]

        def wide(b):
            return ps[:, 512 * b:512 * b + T]

        def over_chunks(ap):
            return ap.unsqueeze(1).to_broadcast([128, NT, ap.shape[1]])

        def halves(ap, b, s):
            return ap.rearrange("p (c q s b) -> p c q s b", c=ap.shape[1] // 128, s=2, b=b)[:, :, :, s, :]

        def ringslot(i):
            return ring[:, (i % RING) * 1024:(i % RING + 1) * 1024]

        w_full = [sem(f"w_full{i}") for i in range(RING)]
        w_used = sem("w_used")
        consts_in, x_in, x_ready = sem("consts_in"), sem("x_in"), sem("x_ready")
        y_stored, sc_tanh, sc_done = sem("y_stored"), sem("sc_tanh"), sem("sc_done")
        pre_step = sem("pre_step")
        begun = sem("begun")
        par_in, win_in, inv_in, cache_in = (sem(n) for n in ("par_in", "win_in", "inv_in", "cache_in"))
        tab_in = [sem(f"tab_in{i}") for i in range(2)]
        TAB_LOADS = (3, 2)
        s0_in = [sem(f"s0_in{i}") for i in range(2)]
        kv_stored = sem("kv_stored")
        fin_stored = [sem(f"fin_stored{i}") for i in range(2)]
        tab_used = signal("tab_used")
        act_step, dve_step, layer_over = signal("act_step"), signal("dve_step"), signal("layer_over")
        act_phase, dve_phase = signal("act_phase"), signal("dve_phase")
        z_free = [signal(f"z_free{i}") for i in range(2)]
        hid_full, arg_ready, hid_ready = signal("hid_full"), signal("arg_ready"), signal("hid_ready")
        filt_copied = signal("filt_copied")
        filt_full, filt_read = signal("filt_full"), signal("filt_read")
        mod_row, mod_cols, mod_done, gate_cols = (signal(n) for n in ("mod_row", "mod_cols", "mod_done", "gate_cols"))
        sq_ready, sq_used, rt_ready = signal("sq_ready"), signal("sq_used"), signal("rt_ready")
        xn_ready, h_ready = signal("xn_ready"), signal("h_ready")
        lin_ready, p_ready, pT_full, pT_ready = signal("lin_ready"), signal("p_ready"), signal("pT_full"), signal("pT_ready")
        H_full, H_ready, U_read, conv_full, conv_read = (signal(n) for n in ("H_full", "H_ready", "U_read", "conv_full", "conv_read"))
        tanh_ready = signal("tanh_ready")
        rot_full, qk_done, v_done, kP_ready, rms_full, rms_rt = (signal(n) for n in ("rot_full", "qk_done", "v_done", "kP_ready", "rms_full", "rms_rt"))
        q_zero = signal("q_zero")
        rms_sq, zn_ready = signal("rms_sq"), signal("zn_ready")
        s_full, s_max, e_ready, pd_ready, pT2_full, pT2_read, pv_full, o_ready = (signal(n) for n in (
            "s_full", "s_max", "e_ready", "pd_ready", "pT2_full", "pT2_read", "pv_full", "o_ready"))
        osq_ready, oss_full, ort_ready = signal("osq_ready"), signal("oss_full"), signal("ort_ready")
        lam_ready, lam_exp, onorm_done = signal("lam_ready"), signal("lam_exp"), signal("onorm_done")
        k_ready, tw_lin, al_ready = (signal(n) for n in ("k_ready", "tw_lin", "al_ready"))
        lora_copied, tw_ready, kk_sq, kk_ss, kk_rt, v_ready = (signal(n) for n in (
            "lora_copied", "tw_ready", "kk_sq", "kk_ss", "kk_rt", "v_ready"))
        vT_full, vT_ready, la_full, th_ready, E_ready, ex_ready = (signal(n) for n in (
            "vT_full", "vT_ready", "la_full", "th_ready", "E_ready", "ex_ready"))
        BK_ready, BT_full, BT_ready, A_full, A_read, ones_ready, T_ready, TT_ready = (signal(n) for n in (
            "BK_ready", "BT_full", "BT_ready", "A_full", "A_read", "ones_ready", "T_ready", "TT_ready"))
        Y_full, Y_ready, D_full = signal("Y_full"), signal("Y_ready"), signal("D_full")
        X_full, X_ready, U2_full, U2_ready, M_full, M_ready, Yt_full, Yt_read = (signal(n) for n in (
            "X_full", "X_ready", "U2_full", "U2_ready", "M_full", "M_ready", "Yt_full", "Yt_read"))
        fin_ready, mu_full, mu_sub, gsq_ready, gss_full, grt_ready, yb_ready, AR_ready = (signal(n) for n in (
            "fin_ready", "mu_full", "mu_sub", "gsq_ready", "gss_full", "grt_ready", "yb_ready", "AR_ready"))
        br_full, br_read, merged_ready, out_read = (signal(n) for n in ("br_full", "br_read", "merged_ready", "out_read"))

        first, last = per_layer[0].num, per_layer[-1].num
        assert [p.num for p in per_layer] == list(range(first, last + 1))

        block = ctx.enter_context(nc.Block())

        @block.sync
        def _(sp):
            for s in range(RING):
                sp.dma_start(ringslot(s), A["w"][s, :, :]).then_inc(w_full[s], 16)
            sp.dma_start(x[:, :], A["x"][:, :]).then_inc(x_in, 16)
            with sp.Fori(0, DEPTH * NSLOT // RING - 1) as g:
                for s in range(RING):
                    sp.wait_ge(w_used, g * RING + (s + 1))
                    sp.dma_start(ringslot(s), A["w"][bass.ds(g * RING + (RING + s), 1), :, :].rearrange("a p n -> (a p) n")).then_inc(w_full[s], 16)

        @block.gpsimd
        def _(pool):
            pool.dma_start(cst[:, :], A["cst"][:, :]).then_inc(consts_in, 16)
            with pool.Fori(0, DEPTH) as l:
                pool.wait_ge(x_ready, l + 1)
                pool.sem_inc(begun, 1)

                def layer(a):
                    return a[bass.ds(l, 1), :, :].rearrange("a p n -> (a p) n")

                pool.dma_start(par[:, :], layer(A["par"])).then_inc(par_in, 16)
                pool.dma_start(yc[:, :], A["win"][:, :]).then_inc(win_in, 16)
                for f, (o, L) in enumerate(TABF):
                    if f >= 2:
                        pool.wait_ge(tab_used, f - 1)
                    pool.dma_start(tab[f % 2][:, 0:2 * L], A["tab"][:, o:o + 2 * L]).then_inc(tab_in[f % 2], 16)
                pool.wait_ge(tab_used, NT)
                pool.dma_start(invt, A["inv"][:, :]).then_inc(inv_in, 16)
                pool.wait_ge(dve_phase, 1)
                pool.wait_ge(act_phase, 1)
                pool.dma_start(t3(kb, T)[:, :, S:T], layer(A["ck"]).rearrange("p (a n) -> p a n", n=P)).then_inc(cache_in, 16)
                pool.dma_start(vC, layer(A["cv"])).then_inc(cache_in, 16)
                nc.gpsimd.memset(qb[0][64:128, :], 0.0).then_inc(q_zero, 1)
                nc.gpsimd.memset(qb[1][0:64, :], 0.0).then_inc(q_zero, 1)
                pool.wait_ge(kP_ready, HEADS)
                pool.dma_start(layer(A["new_k"]), kP).then_inc(kv_stored, 16)
                pool.wait_ge(v_done, JT)
                pool.dma_start(layer(A["new_v"]), t3(vt, BR)[:, NT - 1, :]).then_inc(kv_stored, 16)
                pool.wait_ge(kv_stored, l * 32 + 32)
                pool.sem_inc(begun, 1)
                pool.wait_ge(dve_phase, 2)
                pool.wait_ge(act_phase, 2)
                for g in range(2 * JT):
                    if g >= 2:
                        pool.wait_ge(fin_ready, g - 1)
                        pool.dma_start(A["new_s"][bass.ds(l, 1), :, (g - 2) * 64:(g - 1) * 64].rearrange("a p n -> (a p) n"),
                                       Fin[g % 2]).then_inc(fin_stored[g % 2], 16)
                    pool.dma_start(S0[g % 2], A["s0"][bass.ds(l, 1), :, g * 64:(g + 1) * 64].rearrange("a p n -> (a p) n")).then_inc(s0_in[g % 2], 16)
                for g in range(2 * JT, 2 * JT + 2):
                    pool.wait_ge(fin_ready, g - 1)
                    pool.dma_start(A["new_s"][bass.ds(l, 1), :, (g - 2) * 64:(g - 1) * 64].rearrange("a p n -> (a p) n"),
                                   Fin[g % 2]).then_inc(fin_stored[g % 2], 16)
                for b in range(2):
                    pool.wait_ge(fin_stored[b], l * (16 * JT) + 16 * JT)
                pool.sem_inc(layer_over, 1)
            pool.wait_ge(x_ready, DEPTH + 1)
            pool.dma_start(A["y"][:, :], x[:, :]).then_inc(y_stored, 16)
            pool.wait_ge(y_stored, 16)

        @block.tensor
        def _(pe):
            def mm(out, lhsT, rhs, start, stop):
                return nc.tensor.matmul(out, lhsT, rhs, start=start, stop=stop)

            def wide_mm(b, lhsT, rhs, start=True, stop=True, rows=None):
                o = wide(b) if rows is None else ps[rows, 512 * b:512 * b + T]
                mm(o[:, 0:S], lhsT, rhs[:, 0:S], start, stop)
                return mm(o[:, S:T], lhsT, rhs[:, S:T], start, stop)

            pe.wait_ge(consts_in, 16)
            pe.wait_ge(sc_done, 1)
            with pe.Fori(0, DEPTH) as l:
                pe.wait_ge(x_ready, l + 1)
                pe.sem_inc(begun, 1)

                def weights(*key):
                    i = ORDER.index(key)
                    pe.wait_ge(w_full[i % RING], l * (16 * NSLOT // RING) + 16 * (i // RING + 1))
                    return ringslot(i)

                def z_tile(name, tokens_first=False, first_marks=False):
                    n = ZORDER.index(name)
                    w = weights("z", name)
                    if n >= 2:
                        pe.wait_ge(z_free[n % 2], n // 2)
                    b = 2 * (n % 2)
                    if tokens_first:
                        for t in range(NT):
                            for k in range(KD):
                                i = mm(wide(b)[:, t * 128:(t + 1) * 128], ht(k)[:, t * 128:(t + 1) * 128],
                                       w[:, k * 128:(k + 1) * 128], k == 0, k == KD - 1)
                    else:
                        for k in range(KD):
                            for lo, hi in ((0, S), (S, T)):
                                i = mm(wide(b)[:, lo:hi], w[:, k * 128:(k + 1) * 128], ht(k)[:, lo:hi], k == 0, k == KD - 1)
                                if first_marks and k == 0 and lo == 0:
                                    i.then_inc(w_used, 1)
                    i.then_inc(w_used, 1)

                w = weights("filt",)
                pe.sem_inc(begun, 1)
                feat = con("feat")
                fw = lora

                def modulation(n, quarters=range(4)):
                    for q in quarters:
                        w = weights("ada", n, q)
                        if q == 0 and n >= 2:
                            pe.wait_ge(mod_row, n - 1)
                        for kk in range(2):
                            k = 2 * q + kk
                            i = mm(ps[0:2, 1024 + 512 * (n % 2):1536 + 512 * (n % 2)], sc[:, 2 * k:2 * k + 2], w[:, kk * 512:(kk + 1) * 512],
                                   k == 0, k == KD - 1)
                            if n == 0 and q == 0 and kk == 0:
                                i.then_inc(w_used, 1)
                        i.then_inc(w_used, 1)

                def filters(t):
                    b = 4 + 2 * (t % 2)
                    if t >= 2:
                        pe.wait_ge(filt_read, t - 1)
                    for s in range(2):
                        i = mm(ps[:, 512 * (b + s):512 * (b + s + 1)], hid[0:64, t * 128:(t + 1) * 128],
                               fw[0:64, s * 512:(s + 1) * 512], True, True)
                    i.then_inc(filt_full, 1)

                def turn_rows(first, past, at):
                    for i_ in range(first, past):
                        row = (modrow if i_ < 16 else modrow2)[0:2, (i_ % 16) * 128:(i_ % 16) * 128 + 128]
                        i = nc.tensor.transpose(ps[:, at + 2 * i_:at + 2 * i_ + 2], row, ident[0:2, 0:2])
                    return i

                wide_mm(4, w[64:64 + HY_EMB, 64:128], feat[64:64 + HY_EMB, :], rows=slice(64, 128)).then_inc(hid_full, 1)
                pe.wait_ge(filt_copied, 1)
                modulation(0)
                pe.wait_ge(hid_ready, 1)
                wide_mm(6, fw[64:128, 0:64], hid[64:128, :], rows=slice(0, 64)).then_inc(hid_full, 1)
                for k in range(KD):
                    pe.wait_ge(sq_ready, k + 1)
                    i = wide_mm(0, ones, u_v[k % 2], k == 0, k == KD - 1)
                    i.then_inc(sq_used, 1)
                pe.wait_ge(hid_ready, 2)
                filters(0)
                filters(1)
                modulation(1)
                filters(2)
                modulation(2, (0, 1))
                filters(3)
                modulation(2, (2, 3))
                filters(4)
                modulation(3)
                pe.wait_ge(rt_ready, 1)
                pe.wait_ge(mod_row, 4)
                turn_rows(0, 16, 512).then_inc(mod_cols, 1)
                modulation(4)
                modulation(5)
                pe.wait_ge(filt_read, NT)
                pe.wait_ge(mod_row, 6)
                turn_rows(16, 24, 3072).then_inc(gate_cols, 1)
                pe.wait_ge(mod_done, 1)
                for k in range(KD):
                    pe.wait_ge(h_ready, k + 1)

                def turn_p(j):
                    pe.wait_ge(p_ready, j + 1)
                    if j >= 2:
                        pe.wait_ge(pT_ready, j - 1)
                    b = 4 + 2 * (j % 2)
                    for t in range(NT):
                        i = nc.tensor.transpose(wide(b)[:, t * 128:(t + 1) * 128], tile(p_in, j)[:, t * 128:(t + 1) * 128], ident)
                    i.then_inc(pT_full, 1)

                for j in range(JT):
                    z_tile(f"hv{j}")
                    z_tile(f"hx{j}")
                    if j >= 1:
                        turn_p(j - 1)
                pe.wait_ge(pT_ready, JT - 1)
                for f, (o, L) in enumerate(TABF):
                    pe.wait_ge(tab_in[f % 2], l * (16 * TAB_LOADS[f % 2]) + 16 * (f // 2 + 1))
                    n = L // 128
                    t0 = 0 if f < 4 else NT - 1
                    w = tab[f % 2]
                    if f >= 1:
                        pe.wait_ge(H_ready, f)
                    for s, src in ((0, hs), (1, hd)):
                        for t in range(n):
                            i = mm(ps[:, 512 * (4 + s):512 * (5 + s)], w[:, s * L + t * 128:s * L + (t + 1) * 128],
                                   src[:, (t0 + t) * S:(t0 + t + 1) * S], t == 0, t == n - 1)
                    i.then_inc(H_full, 1)
                    if f == 0:
                        turn_p(JT - 1)
                        pe.wait_ge(pT_ready, JT)
                    if f >= 1:
                        pe.wait_ge(U_read, f)
                    for s in range(2):
                        for t in range(n):
                            i = mm(ps[:, 512 * (6 + s):512 * (7 + s)], w[:, s * L + t * 128:s * L + (t + 1) * 128],
                                   yb[:, (t0 + t) * S:(t0 + t + 1) * S], t == 0, t == n - 1)
                    i.then_inc(tab_used, 1)
                for j in range(JT):
                    z_tile(f"hy{j}")
                    z_tile(f"hg{j}")
                    b = 4 + 2 * (j % 2)
                    if j == 0:
                        pe.wait_ge(inv_in, l * 16 + 16)
                        pe.wait_ge(U_read, NT)
                    if j >= 2:
                        pe.wait_ge(conv_read, j - 1)
                    for f in range(4):
                        for s, src in ((0, yre), (1, yim)):
                            mm(wide(b)[:, 0:S], src[:, f * S + j * 128:f * S + (j + 1) * 128],
                               invt[:, f * TABW + s * S:f * TABW + (s + 1) * S], f == 0 and s == 0, f == 3 and s == 1)
                    for s, src in ((0, yre), (1, yim)):
                        i = mm(wide(b)[:, S:T], src[:, 4 * S + j * 128:4 * S + (j + 1) * 128],
                               invt[:, 4 * TABW + s * P:4 * TABW + (s + 1) * P], s == 0, s == 1)
                    i.then_inc(conv_full, 1)

                def qk_norm(n):
                    pe.wait_ge(rms_sq, n + 1)
                    if n >= 1:
                        pe.wait_ge(rms_rt, n)
                    else:
                        pe.wait_ge(conv_read, JT)
                    wide_mm(4, bones, sq[n % 2]).then_inc(rms_full, 1)

                def qk_rotate(n):
                    pe.wait_ge(zn_ready, n + 1)
                    if n >= 2:
                        pe.wait_ge(qk_done, n - 1)
                    mm(ps[:, 512 * (6 + n % 2):512 * (7 + n % 2)], con("rot"), zn[n % 2][:, 0:S], True, True).then_inc(rot_full, 1)

                values_and_gates = [f"av{j}" for j in range(JT)] + [f"ag{j}" for j in range(JT)]
                for n in range(2 * JT):
                    z_tile(("aq", "ak")[n % 2] + str(n // 2))
                    if n >= 1:
                        qk_norm(n - 1)
                    if n >= 2:
                        qk_rotate(n - 2)
                for n, name in enumerate(values_and_gates):
                    z_tile(name, tokens_first=n < JT)
                    if n == 0:
                        qk_norm(2 * JT - 1)
                        qk_rotate(2 * JT - 2)
                    if n == 1:
                        qk_rotate(2 * JT - 1)
                nz = ZORDER.index("wl")
                for b in range(2):
                    pe.wait_ge(z_free[b], (nz - b + 1) // 2)
                pe.wait_ge(qk_done, 2 * JT)
                pe.wait_ge(cache_in, l * 32 + 32)
                pe.wait_ge(q_zero, 2)
                units = [(hd_, q) for hd_ in range(HEADS) for q in range(NT)]

                def scores(u):
                    hd_, q = units[u]
                    if u >= 2:
                        pe.wait_ge(e_ready, u - 1)
                    base = 1536 * (u % 2)
                    for m in range(2):
                        qq = tile(qb[m], hd_)[:, q * 128:(q + 1) * 128]
                        if q < 4:
                            kk = tile(kb, hd_)
                            cut = 512 - (m * T) % 512
                            mm(ps[:, base + m * T:base + m * T + cut], qq, kk[:, 0:cut], True, True)
                            i = mm(ps[:, base + m * T + cut:base + (m + 1) * T], qq, kk[:, cut:T], True, True)
                        else:
                            i = mm(ps[:, base + m * P:base + (m + 1) * P], qq, kP[:, hd_ * P:(hd_ + 1) * P], True, True)
                    i.then_inc(s_full, 1)

                def turn_pd(u):
                    hd_, q = units[u]
                    pe.wait_ge(pd_ready, u + 1)
                    if u >= 1:
                        pe.wait_ge(pT2_read, u)
                    if q == 0 and hd_ >= 1:
                        pe.wait_ge(o_ready, 2 * hd_)
                    for t in range(5 if q < 4 else 1):
                        i = nc.tensor.transpose(wide(6)[:, t * 128:(t + 1) * 128], pd[u % 2][:, t * 128:(t + 1) * 128], ident)
                    i.then_inc(pT2_full, 1)

                def weigh(hd_):
                    pe.wait_ge(pT2_read, NT * hd_ + 4)
                    if hd_ >= 1:
                        pe.wait_ge(o_ready, 2 * hd_ - 1)
                    for t in range(5):
                        vv = t3(vt, BR)[:, t, :] if t < 4 else vC
                        i = mm(ps[:, 3584:4096], vv[:, hd_ * 128:(hd_ + 1) * 128], pdT[:, t * S:(t + 1) * S], t == 0, t == 4)
                    i.then_inc(pv_full, 1)

                def weigh_ctx(hd_):
                    pe.wait_ge(pT2_read, NT * hd_ + 5)
                    mm(ps[:, 3200:3328], t3(vt, BR)[:, 4, hd_ * 128:(hd_ + 1) * 128], pctx,
                       True, True).then_inc(pv_full, 1)

                pctx = rope[0][:, 0:128]
                scores(0)
                scores(1)
                for u in range(len(units)):
                    if u + 2 < len(units):
                        scores(u + 2)
                    hd_, q = units[u]
                    turn_pd(u)
                    if q == 3:
                        weigh(hd_)
                    if q == 4:
                        weigh_ctx(hd_)
                def head_sums(hd_):
                    pe.wait_ge(osq_ready, hd_ + 1)
                    if hd_ < 2:
                        pe.wait_ge(o_ready, 2 * HEADS)
                    else:
                        pe.wait_ge(ort_ready, hd_ - 1)
                    wide_mm(4 + 2 * (hd_ % 2), ones, sq[hd_ % 2]).then_inc(oss_full, 1)

                pe.wait_ge(e_ready, len(units))
                pe.wait_ge(lora_copied, 1)
                z_tile("wl", first_marks=True)
                head_sums(0)
                head_sums(1)
                z_tile("al")
                head_sums(2)
                head_sums(3)

                def norm_sums(j):
                    pe.wait_ge(Yt_read, 2 * j + 2)
                    wide_mm(6, bones, tile(yb, j))
                    wide_mm(4, bones, tC[5]).then_inc(mu_full, 1)

                def norm_squares(j):
                    pe.wait_ge(gsq_ready, j + 1)
                    wide_mm(6, bones, tC[1]).then_inc(gss_full, 1)

                def low_rank(j, d):
                    rows = slice(64 * d, 64 * d + 64)
                    wide_mm(4, lora[rows, j * 128:(j + 1) * 128], tw[rows, :])
                    wide_mm(6, lora[rows, 512 + j * 128:512 + (j + 1) * 128], tal[rows, :]).then_inc(la_full, 1)

                for j in range(JT):
                    z_tile(f"rk{j}")
                    if j >= 1:
                        norm_sums(j - 1)
                    z_tile(f"rr{j}")
                    if j >= 1:
                        norm_squares(j - 1)
                        pe.wait_ge(mu_sub, j)
                    if j == 0:
                        pe.wait_ge(ort_ready, HEADS)
                    pe.wait_ge(kk_sq, j + 1)
                    wide_mm(4, bones, kksq).then_inc(kk_ss, 1)
                    z_tile(f"rv{j}")
                    if j == 0:
                        pe.wait_ge(tw_ready, 1)
                        pe.wait_ge(al_ready, 1)
                    else:
                        pe.wait_ge(grt_ready, j)
                    pe.wait_ge(kk_rt, j + 1)
                    low_rank(j, 0)
                    z_tile(f"rg{j}")
                    pe.wait_ge(th_ready, 2 * j + 1)
                    low_rank(j, 1)
                    pe.wait_ge(v_ready, j + 1)
                    pe.wait_ge(th_ready, 2 * j + 2)
                    for t in range(NT):
                        i = nc.tensor.transpose(wide(6)[:, t * 128:(t + 1) * 128], v_[:, t * 128:(t + 1) * 128], ident)
                    i.then_inc(vT_full, 1)
                    nzj = ZORDER.index(f"rg{j}") + 1
                    for d in range(2):
                        g = 2 * j + d
                        pe.wait_ge(BK_ready, g + 1)
                        if d == 0:
                            pe.wait_ge(vT_ready, j + 1)
                        for b, src in ((6, Kt), (4, Bt)):
                            if d == 1 and b == 4:
                                pe.wait_ge(Yt_read, g)
                            for t in range(NT):
                                i = nc.tensor.transpose(wide(b)[:, t * 128:(t + 1) * 128], src[:, t * 128:(t + 1) * 128], ident)
                        i.then_inc(BT_full, 1)
                        pe.wait_ge(AR_ready, g + 1)
                        if d == 0:
                            for b in range(2):
                                pe.wait_ge(z_free[b], (nzj - b + 1) // 2)
                        for hh in range(2):
                            hr = slice(64 * hh, 64 * hh + 64)
                            for part in range(3):
                                n = 6 * g + 3 * hh + part
                                if hh == 0 and part == 1:
                                    pe.wait_ge(BT_ready, g + 1)
                                if hh == 1:
                                    pe.wait_ge(A_read, n - 2)
                                for c in range(NT):
                                    cc = slice(c * 128, (c + 1) * 128)
                                    if part < 2:
                                        o = 1536 * part + c * 256
                                        i = mm(ps[:, o:o + 256], (Bt, Kt)[part][hr, cc], AR[hr, c * 256:(c + 1) * 256], True, True)
                                    else:
                                        i = mm(wide(6)[:, cc], AR[hr, c * 256:c * 256 + 128], Bt[hr, cc], True, True)
                                i.then_inc(A_full, 1)
                        for lev in range(6):
                            n = 6 * g + lev
                            last_level = lev == 5
                            for hh in range(2):
                                pe.wait_ge(TT_ready, 2 * (7 * g + lev) + hh + 1)
                                pe.wait_ge(T_ready, 2 * (6 * g + lev) + hh + 1)
                                if lev == 0 and hh == 0:
                                    pe.wait_ge(A_read, 6 * g + 6)
                                for c in range(NT):
                                    cc = slice(c * 128, (c + 1) * 128)
                                    i = mm(wide(4 * hh)[:, cc], ABQ[hh][:, c * 256:c * 256 + 128], Tm[hh][:, cc], True, True)
                                i.then_inc(Y_full, 1)
                            for part in (1,) if last_level else (0, 1):
                                for hh in range(2):
                                    if part == 0 or last_level:
                                        pe.wait_ge(Y_ready, 2 * n + hh + 1)
                                    for c in range(NT):
                                        cc = slice(c * 128, (c + 1) * 128)
                                        if part == 0:
                                            i = mm(wide(4 * hh + 2)[:, cc], TT[hh][:, cc], Ysb[hh][:, cc], True, True)
                                        else:
                                            i = mm(wide(4 * hh)[:, cc], Ysb[hh][:, cc], TT[hh][:, cc], True, True)
                                    i.then_inc(D_full, 1)
                        pe.wait_ge(TT_ready, 14 * (g + 1))
                        order = [4] + ([0, 1, 2, 3] if d == 0 else [3, 2, 1, 0])
                        heads_of_tile = [(hh, slice(64 * hh, 64 * hh + 64)) for hh in range(2)]

                        def x_of_values(c, stop):
                            for hh, hr in heads_of_tile:
                                i = mm(ps[:, 512 * hh:512 * hh + 64], AKQ[hh][:, c * 256:c * 256 + 128],
                                       vtok[:, c * 128 + 64 * hh:c * 128 + 64 * hh + 64], True, stop)
                            return i

                        def outputs_of(n, part):
                            c = order[n]
                            for hh, hr in heads_of_tile:
                                tc_ = slice(c * 128 + 64 * hh, c * 128 + 64 * hh + 64)
                                o = ps[hr, 2048 + c * 128:2048 + (c + 1) * 128]
                                if part == 0:
                                    i = mm(o, vtok[:, tc_], AKQ[hh][:, c * 256 + 128:(c + 1) * 256], True, False)
                                elif part == 1:
                                    i = mm(o, Ms[n % 2][hr, :], AR[hr, c * 256 + 128:(c + 1) * 256], False, False)
                                else:
                                    i = mm(o, Us[n % 2][:, 64 * hh:64 * hh + 64], ABQ[hh][:, c * 256 + 128:(c + 1) * 256], False, True)
                            return i

                        x_of_values(order[0], True).then_inc(X_full, 1)
                        for n, c in enumerate(order):
                            ns = 5 * g + n
                            cc = slice(c * 128, (c + 1) * 128)
                            M, Un = Ms[n % 2], Us[n % 2]
                            if n >= 1:
                                pe.wait_ge(M_ready, ns + 1)
                                for hh, hr in heads_of_tile:
                                    i = mm(ps[:, 512 * hh:512 * hh + 64], AR[hr, c * 256:c * 256 + 128], M[hr, :], False, True)
                                i.then_inc(X_full, 1)
                            for hh, hr in heads_of_tile if n < 4 else ():
                                tc_ = slice(c * 128 + 64 * hh, c * 128 + 64 * hh + 64)
                                mm(ps[hr, 1024:1088], Ktok[:, tc_], vtok[:, tc_], True, False)
                                if n:
                                    mm(ps[hr, 1024:1088], ident[hr, hr], M[hr, :], False, False)
                            if n:
                                outputs_of(n - 1, 2)
                            pe.wait_ge(X_ready, ns + 1)
                            for hh in range(2):
                                i = mm(ps[:, 1536 + 64 * hh:1536 + 64 * hh + 64], TT[hh][:, cc], Xs[n % 2][:, 64 * hh:64 * hh + 64], True, True)
                            i.then_inc(U2_full, 1)
                            if n < 4:
                                x_of_values(order[n + 1], False)
                            outputs_of(n, 0)
                            pe.wait_ge(U2_ready, ns + 1)
                            if n < 4:
                                for hh, hr in heads_of_tile:
                                    tc_ = slice(c * 128 + 64 * hh, c * 128 + 64 * hh + 64)
                                    i = mm(ps[hr, 1024:1088], Btok[:, tc_], Un[:, 64 * hh:64 * hh + 64], False, True)
                                i.then_inc(M_full, 1)
                            if n:
                                outputs_of(n, 1)
                        i = outputs_of(4, 2)
                        i.then_inc(Yt_full, 1)

                for p in range(KD // 2):
                    for b in range(3):
                        z_tile(f"m{b}{2 * p}")
                        if p == 0 and b == 0:
                            norm_sums(JT - 1)
                        z_tile(f"m{b}{2 * p + 1}")
                        if p == 0 and b == 0:
                            norm_squares(JT - 1)
                            pe.wait_ge(mu_sub, JT)
                            pe.wait_ge(grt_ready, JT)
                        if p == 0 and b == 1:
                            pe.wait_ge(yb_ready, JT)
                        w = weights("br", p, b)
                        for jj in range(2):
                            n = 6 * p + 2 * b + jj
                            if n >= 2:
                                pe.wait_ge(br_read, n - 1)
                            for k in range(JT):
                                i = wide_mm(4 + 2 * jj, w[:, (jj * JT + k) * 128:(jj * JT + k + 1) * 128], tile((ya, yb, yc)[b], k), k == 0, k == JT - 1)
                            i.then_inc(br_full if jj == 0 else w_used, 1)
                pe.wait_ge(merged_ready, KD)
                for j in range(KD):
                    w = weights("out", j)
                    if j >= 2:
                        pe.wait_ge(out_read, j - 1)
                    for k in range(KD):
                        i = wide_mm(4 + 2 * (j % 2), w[:, k * 128:(k + 1) * 128], tile(mg, k), k == 0, k == KD - 1)
                    i.then_inc(w_used, 1)
                pe.sem_inc(layer_over, 1)

        def used(key):
            return ORDER.index(key) + 1

        @block.scalar
        def _(act):
            step = Steps(act, act_step)
            A_ = nc.scalar.activation
            act.wait_ge(consts_in, 16)
            A_(sc[:, :], con("c"), ACT.Tanh, scale=0.5).then_inc(sc_tanh, 1)
            with act.Fori(0, DEPTH) as l:
                act.wait_ge(x_ready, l + 1)
                act.sem_inc(begun, 1)
                act.wait_ge(par_in, l * 16 + 16)

                def z_full(name):
                    act.wait_ge(w_used, l * NSLOT + used(("z", name)))
                    return wide(2 * (ZORDER.index(name) % 2))

                act.wait_ge(w_full[0], l * (16 * NSLOT // RING) + 16)
                A_(lora[:, :], ringslot(0), ACT.Copy).then_inc(filt_copied, 1)

                def square(k):
                    if k >= 2:
                        act.wait_ge(sq_used, k - 1)
                    A_(u_v[k % 2], xt(k), ACT.Square).then_inc(sq_ready, 1)

                def sine(n):
                    rows = (slice(64, 128), slice(0, 64))[n]
                    act.wait_ge(arg_ready, n + 1)
                    A_(hid[rows, :], tA[0][rows, :], ACT.Sin).then_inc(hid_ready, 1)

                def copy_row(n):
                    act.wait_ge(w_used, l * NSLOT + used(("ada", n, 3)))
                    dst = (modrow if n < 4 else modrow2)[0:2, (n % 4) * 512:(n % 4 + 1) * 512]
                    A_(dst, ps[0:2, 1024 + 512 * (n % 2):1536 + 512 * (n % 2)], ACT.Copy).then_inc(mod_row, 1)

                act.wait_ge(x_in, 16)
                square(0)
                square(1)
                sine(0)
                copy_row(0)
                for k in range(2, KD):
                    square(k)
                sine(1)
                act.wait_ge(sq_used, KD)
                A_(u_x[0], wide(0), ACT.Sqrt, scale=1.0 / D, bias=eps(EPS_NORM)).then_inc(rt_ready, 1)
                for n in range(1, 4):
                    copy_row(n)
                act.wait_ge(mod_done, 1)
                for k in range(KD):
                    act.wait_ge(xn_ready, k + 1)
                    for s, (lo, hi) in enumerate(((0, S), (S, T))):
                        i = A_(ht(k)[:, lo:hi], tA[2 + k % 2][:, lo:hi], ACT.Identity, scale=dcol("A", 2 * k + s), bias=dcol("B", 2 * k + s))
                        if s == 0:
                            i.then_inc(step.next(), 1)
                    i.then_inc(h_ready, 1)
                    if k == 3:
                        copy_row(4)
                copy_row(5)

                def lin(name, dst, w1, b):
                    z = z_full(name)
                    A_(dst, z, ACT.Identity, scale=w1, bias=b).then_inc(lin_ready, 1)

                def turned_p(j):
                    act.wait_ge(pT_full, j + 1)
                    A_(t3(yb[:, :], S)[:, :, j * 128:(j + 1) * 128], t3(wide(4 + 2 * (j % 2)), 128), ACT.Copy).then_inc(pT_ready, 1)

                for j in range(JT):
                    if j >= 2:
                        act.wait_ge(p_ready, j - 1)
                    lin(f"hv{j}", u_v[j % 2], pcol("cw1", j), pcol("cb", j))
                    lin(f"hx{j}", u_x[j % 2], pcol("cw1", 8 + j), pcol("cb", 8 + j))
                    if j >= 1:
                        turned_p(j - 1)
                turned_p(JT - 1)
                for f in range(NT):
                    act.wait_ge(H_full, f + 1)
                    if f >= 2:
                        act.wait_ge(U_read, f - 1)
                    A_(Hre[f % 2], ps[:, 2048:2560], ACT.Copy).then_inc(step.next(), 1)
                    A_(Him[f % 2], ps[:, 2560:3072], ACT.Copy).then_inc(H_ready, 1)
                for j in range(JT):
                    if j == 0:
                        act.wait_ge(p_ready, JT)
                    if j >= 2:
                        act.wait_ge(conv_read, j - 1)
                    lin(f"hy{j}", u_v[j % 2], pcol("cw1", 4 + j), pcol("cb", 4 + j))
                    A_(u_x[j % 2], z_full(f"hg{j}"), ACT.Tanh, scale=0.5).then_inc(tanh_ready, 1)
                act.wait_ge(tanh_ready, JT)
                act.sem_inc(act_phase, 1)
                act.wait_ge(dve_phase, 1)

                def qk_root(n):
                    act.wait_ge(rms_full, n + 1)
                    if n >= 2:
                        act.wait_ge(zn_ready, n - 1)
                    A_(rr[n % 2], wide(4), ACT.Sqrt, scale=1.0 / DH, bias=eps(EPS_NORM)).then_inc(rms_rt, 1)

                for n in range(2 * JT):
                    z = z_full(("aq", "ak")[n % 2] + str(n // 2))
                    if n >= 2:
                        act.wait_ge(zn_ready, n - 1)
                        act.wait_ge(rms_full, n - 1)
                    A_(zc[n % 2], z, ACT.Copy).then_inc(step.next(), 1)
                    A_(sq[n % 2], z, ACT.Square).then_inc(rms_sq, 1)
                    act.wait_ge(rms_sq, n + 1)
                    act.sem_inc(z_free[ZORDER.index(("aq", "ak")[n % 2] + str(n // 2)) % 2], 1)
                    if n >= 1:
                        qk_root(n - 1)
                qk_root(2 * JT - 1)
                for j in range(JT):
                    z = z_full(f"av{j}")
                    A_(t3(vt, BR)[:, :, j * 128:(j + 1) * 128], t3(z, 128), ACT.Copy).then_inc(v_done, 1)
                    act.wait_ge(v_done, j + 1)
                    act.sem_inc(z_free[ZORDER.index(f"av{j}") % 2], 1)
                for j in range(JT):
                    if j >= 2:
                        act.wait_ge(z_free[ZORDER.index(f"ag{j - 2}") % 2], ZORDER.index(f"ag{j - 2}") // 2 + 1)
                    if j == 0:
                        act.wait_ge(zn_ready, 2 * JT)
                    A_(zc[j % 2], z_full(f"ag{j}"), ACT.Tanh, scale=0.5).then_inc(tanh_ready, 1)
                units = [(hd_, q) for hd_ in range(HEADS) for q in range(NT)]
                pctx = rope[0][:, 0:128]

                def exps(u):
                    hd_, q = units[u]
                    act.wait_ge(s_max, u + 1)
                    if u >= 2:
                        act.wait_ge(pd_ready, u - 1)
                    w = T if q < 4 else P
                    for m in range(2):
                        st = stat[:, 8 * (u % 2):8 * (u % 2) + 8]
                        i = A_(eb[u % 2][:, m * T:m * T + w], ps[:, 1536 * (u % 2) + m * w:1536 * (u % 2) + (m + 1) * w], ACT.Exp,
                               bias=st[:, m:m + 1], accum_out=st[:, 2 + m:3 + m])
                        if m == 0:
                            i.then_inc(step.next(), 1)
                    i.then_inc(e_ready, 1)

                def turned_pd(u):
                    hd_, q = units[u]
                    act.wait_ge(pT2_full, u + 1)
                    if q == 0 and hd_ >= 1:
                        act.wait_ge(pv_full, 2 * hd_)
                    if q < 4:
                        A_(t3(pdT, S)[:, :, q * 128:(q + 1) * 128], t3(wide(6), 128), ACT.Copy).then_inc(pT2_read, 1)
                    else:
                        A_(pctx, ps[:, 3072:3200], ACT.Copy).then_inc(pT2_read, 1)

                def outputs(n):
                    hd_ = n // 2
                    act.wait_ge(pv_full, n + 1)
                    if n % 2 == 0:
                        A_(tile(yc, hd_)[:, 0:S], ps[:, 3584:4096], ACT.Copy).then_inc(o_ready, 1)
                    else:
                        A_(tile(yc, hd_)[:, S:T], ps[:, 3200:3328], ACT.Copy).then_inc(o_ready, 1)

                def head_root(n):
                    act.wait_ge(oss_full, n + 1)
                    if n >= 2:
                        act.wait_ge(onorm_done, n - 1)
                    A_(rr[n % 2], wide(4 + 2 * (n % 2)), ACT.Sqrt, scale=1.0 / (2 * DH), bias=eps(EPS_SUB)).then_inc(ort_ready, 1)

                act.wait_ge(lam_ready, 1)
                A_(dcol("ls", 2, 2), dcol("ls", 0, 2), ACT.Exp).then_inc(lam_exp, 1)
                for u in range(len(units)):
                    exps(u)
                    if u >= 1:
                        turned_pd(u - 1)
                        if units[u - 1][1] >= 3:
                            outputs(2 * units[u - 1][0] + units[u - 1][1] - 3)
                turned_pd(len(units) - 1)
                outputs(2 * HEADS - 1)
                act.wait_ge(o_ready, 2 * HEADS)
                i_l = ORDER.index(("lora",))
                act.wait_ge(w_full[i_l % RING], l * (16 * NSLOT // RING) + 16 * (i_l // RING + 1))
                A_(lora[:, :], ringslot(i_l), ACT.Copy).then_inc(lora_copied, 1)

                def head_square(hd_):
                    if hd_ >= 2:
                        act.wait_ge(oss_full, hd_ - 1)
                    A_(sq[hd_ % 2], tile(yc, hd_), ACT.Square).then_inc(osq_ready, 1)

                head_square(0)
                head_square(1)
                lin("wl", tw, dcol("ommu", 12), 0.0)
                head_root(0)
                head_square(2)
                head_root(1)
                head_square(3)
                lin("al", tal, dcol("ommu", 13), 0.0)
                act.wait_ge(tw_lin, 1)
                A_(tw, tw, ACT.Tanh).then_inc(tw_ready, 1)
                head_root(2)
                head_root(3)
                act.wait_ge(ort_ready, HEADS)
                act.sem_inc(act_phase, 1)

                def squared(j):
                    act.wait_ge(mu_sub, j + 1)
                    A_(tC[1], tC[0], ACT.Square).then_inc(gsq_ready, 1)

                def norm_root(j):
                    act.wait_ge(gss_full, j + 1)
                    A_(tC[2], wide(6), ACT.Sqrt, scale=1.0 / 64, bias=eps(EPS_GN)).then_inc(grt_ready, 1)

                def low_rank_tanh(j, d):
                    act.wait_ge(la_full, 2 * j + d + 1)
                    a, b = ((tC[0], tC[5]), th1)[d]
                    A_(a, wide(4), ACT.Tanh, scale=0.5, bias=dcol("hw0", 4 * d + j)).then_inc(step.next(), 1)
                    A_(b, wide(6), ACT.Tanh, scale=0.5, bias=dcol("ha0", 4 * d + j)).then_inc(th_ready, 1)

                E, Em = tC[2], tC[1]

                def decay(g, n):
                    d = g % 2
                    if n == 0:
                        act.wait_ge(E_ready, g + 1)
                        A_(dec[d][:, 0:5], t3(E, 128)[:, :, 127], ACT.Exp, scale=KAPPA).then_inc(step.next(), 1)
                        A_(dec[d][:, 5:10], t3(Em, 128)[:, :, 0], ACT.Exp, scale=-KAPPA).then_inc(step.next(), 1)
                    src, sign = (((E, -1), (E, 1), (Em, 1)), ((Em, 1), (Em, -1), (E, -1)))[d][n]
                    A_((tC[0], tC[3], tC[4])[n], src, ACT.Exp, scale=sign * KAPPA).then_inc(ex_ready, 1)

                for j in range(JT):
                    lin(f"rk{j}", k_, dcol("ommu", 4 + j), 0.0)
                    if j >= 1:
                        squared(j - 1)
                    lin(f"rr{j}", r_, dcol("ommu", j), 0.0)
                    act.wait_ge(k_ready, j + 1)
                    A_(kksq, k_, ACT.Square, scale=pcol("kk", j)).then_inc(kk_sq, 1)
                    if j >= 1:
                        norm_root(j - 1)
                    act.wait_ge(kk_ss, j + 1)
                    A_(kkrt, wide(4), ACT.Sqrt, bias=eps(EPS_KK)).then_inc(kk_rt, 1)
                    if j >= 1:
                        act.wait_ge(yb_ready, j)
                    else:
                        act.wait_ge(dve_phase, 2)
                    lin(f"rv{j}", v_, dcol("ommu", 8 + j), 0.0)
                    low_rank_tanh(j, 0)
                    for n in range(3):
                        decay(2 * j, n)
                    A_(gth, z_full(f"rg{j}"), ACT.Tanh, scale=0.5).then_inc(tanh_ready, 1)
                    low_rank_tanh(j, 1)
                    act.wait_ge(vT_full, j + 1)
                    A_(vtok, wide(6), ACT.Copy).then_inc(vT_ready, 1)
                    for d in range(2):
                        g = 2 * j + d
                        act.wait_ge(BT_full, g + 1)
                        A_(Btok, wide(4), ACT.Copy).then_inc(step.next(), 1)
                        A_(Ktok, wide(6), ACT.Copy).then_inc(BT_ready, 1)
                        for buf in Tm + TT:
                            A_(t3(buf, 128), over_chunks(ident), ACT.Copy).then_inc(ones_ready, 1)
                        if g == 0:
                            for buf in Ysb:
                                A_(t3(buf, 128), over_chunks(ident), ACT.Copy).then_inc(step.next(), 1)
                            step.settle()
                        for lev in range(6):
                            for hh in range(2):
                                n = 2 * (6 * g + lev) + hh
                                b = LEVELS[lev + 1]
                                act.wait_ge(Y_full, n + 1)
                                A_(halves(Ysb[hh], b, d), halves(wide(4 * hh), b, d), ACT.Copy).then_inc(Y_ready, 1)
                            if d == 0 and lev >= 2 and lev < 5:
                                decay(g + 1, lev - 2)
                        for n in range(5):
                            act.wait_ge(X_full, 5 * g + n + 1)
                            A_(t3(Xs[n % 2], 64), t3(ps[:, 0:1024], 512)[:, :, 0:64], ACT.Copy).then_inc(X_ready, 1)
                        if d == 0:
                            act.wait_ge(Yt_full, g + 1)
                            A_(tile(yb, j), wide(4), ACT.Copy).then_inc(Yt_read, 1)
                for n in range(3 * KD):
                    p, b, jj = n // 6, n // 2 % 3, n % 2
                    name = f"m{b}{2 * p + jj}"
                    z = z_full(name)
                    if n >= 2:
                        act.wait_ge(br_read, n - 1)
                    A_(tg[n % 2], z, ACT.Tanh, scale=0.5).then_inc(tanh_ready, 1)
                    act.wait_ge(tanh_ready, 3 * JT + n + 1)
                    act.sem_inc(z_free[ZORDER.index(name) % 2], 1)
                    if n == 0:
                        squared(JT - 1)
                    if n == 1:
                        norm_root(JT - 1)
                act.sem_inc(layer_over, 1)

        @block.vector
        def _(dve):
            step = Steps(dve, pre_step)
            V = nc.vector
            STT, TTn, TS = V.scalar_tensor_tensor, V.tensor_tensor, V.tensor_scalar
            MUL, ADD, SUB = ALU.mult, ALU.add, ALU.subtract
            rs3 = resetm[:, :].rearrange("p (a n) -> p a n", n=128)
            V.memset(resetm[:, :], 1.0).then_inc(step.next(), 1)
            step.settle()
            V.memset(rs3[:, :, 0:1], 0.0).then_inc(step.next(), 1)
            dve.wait_ge(consts_in, 16)
            dve.wait_ge(sc_tanh, 1)
            STT(sc[:, :], sc[:, :], 1.0, con("c"), ADD, MUL).then_inc(step.next(), 1)
            step.settle()
            TS(sc[:, :], sc[:, :], 0.5, None, MUL).then_inc(sc_done, 1)
            dve.sem_inc(x_ready, 1)
            step = Steps(dve, dve_step)
            with dve.Fori(0, DEPTH) as l:
                step.again()
                dve.wait_ge(par_in, l * 16 + 16)

                def do(ins):
                    ins.then_inc(step.next(), 1)

                def link(ins):
                    ins.then_inc(step.next(), 1)
                    step.settle()

                do(TS(dcol("hmu", 0, 14), pcol("mu", 0, 14), 0.5, None, MUL))
                do(TS(dcol("ommu", 0, 14), pcol("mu", 0, 14), -1.0, 1.0, MUL, ADD))
                do(TS(dcol("hw0", 0, 8), pcol("w0", 0, 8), 0.5, None, MUL))
                do(TS(dcol("ha0", 0, 8), pcol("a0", 0, 8), 0.5, None, MUL))
                do(TS(dcol("hka", 0, 4), pcol("ka", 0, 4), 0.5, None, MUL))
                do(TS(dcol("omka", 0, 4), pcol("ka", 0, 4), -0.5, 1.0, MUL, ADD))
                do(TS(dcol("rkh", 0, 4), pcol("rk", 0, 4), 0.5, None, MUL))
                do(TTn(dcol("gsl"), pcol("gsub"), pcol("oneml"), MUL))
                do(TS(dcol("gq8"), pcol("gq"), DH ** -0.5, None, MUL))
                do(TTn(pcol("lq1", 0, 64), pcol("lq1", 0, 64), pcol("lk1", 0, 64), MUL))
                link(TTn(pcol("lq2", 0, 64), pcol("lq2", 0, 64), pcol("lk2", 0, 64), MUL))
                do(V.tensor_reduce(dcol("ls", 0), pcol("lq1", 0, 64), AX.X, ADD))
                V.tensor_reduce(dcol("ls", 1), pcol("lq2", 0, 64), AX.X, ADD).then_inc(lam_ready, 1)

                for n, rows in enumerate((slice(64, 128), slice(0, 64))):
                    dve.wait_ge(hid_full, n + 1)
                    a, c = tA[1][rows, :], tA[2][rows, :]
                    fo, fr = PCOL["fb"][0], PCOL["freq"][0]
                    link(TS(a, ps[rows, 2048 + 1024 * n:2048 + 1024 * n + T], par[rows, fo:fo + 1], par[rows, fr:fr + 1], ADD, MUL))
                    link(TS(c, a, 1.0 / TWO_PI, ROUND, MUL, ADD))
                    link(TS(c, c, ROUND, None, SUB))
                    link(STT(a, c, -PI_HI, a, MUL, ADD))
                    link(STT(a, c, -PI_MID, a, MUL, ADD))
                    link(STT(a, c, -PI_LO, a, MUL, ADD))
                    TS(tA[0][rows, :], a, math.pi * (1 - 1e-7), -math.pi * (1 - 1e-7), ALU.min, ALU.max).then_inc(arg_ready, 1)
                dve.wait_ge(win_in, l * 16 + 16)
                for t in range(NT):
                    b = 2048 + 1024 * (t % 2)
                    dve.wait_ge(filt_full, t + 1)
                    hf, hb = tA[2 * (t % 2)][:, 0:S], tA[2 * (t % 2) + 1][:, 0:S]
                    win = yc[:, t * S:(t + 1) * S]
                    do(TTn(hf, ps[:, b:b + 512], win, MUL))
                    link(TTn(hb, ps[:, b + 512:b + 1024], win, MUL))
                    if t in (0, NT - 1):
                        link(V.memset(hb[0:1, :], 0.0))
                    do(TTn(hs[:, t * S:(t + 1) * S], hf, hb, ADD))
                    link(TTn(hd[:, t * S:(t + 1) * S], hb, hf, SUB))
                    dve.sem_inc(filt_read, 1)
                rstd = u_x[0]
                dve.wait_ge(rt_ready, 1)
                link(V.reciprocal(rstd, rstd))
                dve.wait_ge(mod_cols, 1)
                mod = dcol("mod", 0, 48)
                m3 = mod.rearrange("p (a n) -> p a n", n=2)
                link(TTn(m3[:, 0:16, :], ps[:, 512:544].rearrange("p (a n) -> p a n", n=2), pcol("bada", 0, 16).unsqueeze(2).to_broadcast([128, 16, 2]), ADD))
                do(V.tensor_copy(dcol("B", 0, 16), mod[:, 0:16]))
                link(STT(dcol("A", 0, 16).rearrange("p (a n) -> p a n", n=2), m3[:, 8:16, :], 1.0, pcol("g", 0, 8).unsqueeze(2).to_broadcast([128, 8, 2]), ADD, MUL))
                dve.sem_inc(mod_done, 1)
                dve.wait_ge(x_in, 16)
                for k in range(KD):
                    if k >= 2:
                        dve.wait_ge(h_ready, k - 1)
                    TTn(tA[2 + k % 2], xt(k), rstd, MUL).then_inc(xn_ready, 1)
                dve.wait_ge(gate_cols, 1)
                link(TTn(m3[:, 16:24, :], ps[:, 3104:3120].rearrange("p (a n) -> p a n", n=2), pcol("bada", 16, 8).unsqueeze(2).to_broadcast([128, 8, 2]), ADD))
                do(TS(dcol("gate", 0, 16), mod[:, 32:48], 0.5, None, MUL))

                n_lin = [0]

                def taps(name, u, w0, w2):
                    z = wide(2 * (ZORDER.index(name) % 2))
                    n_lin[0] += 1
                    dve.wait_ge(lin_ready, n_lin[0])
                    do(STT(u[:, 1:S], z[:, 0:S - 1], w0, u[:, 1:S], MUL, ADD))
                    link(STT(u[:, S + 1:T], z[:, S:T - 1], w0, u[:, S + 1:T], MUL, ADD))
                    do(STT(u[:, 0:S - 1], z[:, 1:S], w2, u[:, 0:S - 1], MUL, ADD))
                    link(STT(u[:, S:T - 1], z[:, S + 1:T], w2, u[:, S:T - 1], MUL, ADD))
                    dve.sem_inc(z_free[ZORDER.index(name) % 2], 1)

                n_tanh = [0]

                def silu_of(name, dst, th):
                    z = wide(2 * (ZORDER.index(name) % 2))
                    n_tanh[0] += 1
                    dve.wait_ge(tanh_ready, n_tanh[0])
                    link(STT(dst, th, 1.0, z, ADD, MUL))
                    dve.sem_inc(z_free[ZORDER.index(name) % 2], 1)

                for j in range(JT):
                    taps(f"hv{j}", u_v[j % 2], pcol("cw0", j), pcol("cw2", j))
                    taps(f"hx{j}", u_x[j % 2], pcol("cw0", 8 + j), pcol("cw2", 8 + j))
                    TTn(tile(p_in, j), u_v[j % 2], u_x[j % 2], MUL).then_inc(p_ready, 1)
                for f in range(NT):
                    dve.wait_ge(H_ready, f + 1)
                    dve.wait_ge(tab_used, f + 1)
                    Uc, Us_ = ps[:, 3072:3584], ps[:, 3584:4096]
                    o = slice(f * S, (f + 1) * S)
                    a, b, c, e = (t[:, 0:S] for t in tA)
                    do(TTn(a, Uc, Hre[f % 2], MUL))
                    do(TTn(b, Us_, Him[f % 2], MUL))
                    do(TTn(c, Us_, Hre[f % 2], MUL))
                    link(TTn(e, Uc, Him[f % 2], MUL))
                    do(TTn(yre[:, o], a, b, ADD))
                    link(TTn(yim[:, o], c, e, SUB))
                    dve.sem_inc(U_read, 1)
                for j in range(JT):
                    taps(f"hy{j}", u_v[j % 2], pcol("cw0", 4 + j), pcol("cw2", 4 + j))
                    gate = u_x[j % 2]
                    silu_of(f"hg{j}", gate, gate)
                    dve.wait_ge(conv_full, j + 1)
                    link(STT(tA[0], tile(p_in, j), pcol("hyb", j), wide(4 + 2 * (j % 2)), MUL, ADD))
                    link(TTn(tA[1], tA[0], u_v[j % 2], MUL))
                    link(STT(tile(ya, j), tA[1], 0.5, gate, MUL, MUL))
                    dve.sem_inc(conv_read, 1)
                dve.sem_inc(dve_phase, 1)
                dve.wait_ge(act_phase, 1)

                def normed(n):
                    dve.wait_ge(rms_rt, n + 1)
                    link(V.reciprocal(rr[n % 2], rr[n % 2]))
                    link(STT(zn[n % 2], zc[n % 2], (dcol("gq8"), pcol("gk"))[n % 2], rr[n % 2], MUL, MUL))
                    dve.sem_inc(zn_ready, 1)

                def rotated(n):
                    j = n // 2
                    halves = (slice(0, 64), slice(64, 128))
                    if n % 2 == 0:
                        for m, rows in enumerate(halves):
                            do(V.tensor_copy(tile(qb[m], j)[rows, S:T], zn[n % 2][rows, S:T]))
                    else:
                        link(V.tensor_copy(kP[:, j * P:(j + 1) * P], zn[n % 2][:, S:T]))
                        dve.sem_inc(kP_ready, 1)
                    do(TTn(rope[0], zn[n % 2][:, 0:S], con("cos"), MUL))
                    dve.wait_ge(rot_full, n + 1)
                    link(TTn(rope[1], ps[:, 512 * (6 + n % 2):512 * (7 + n % 2)], con("sin"), MUL))
                    if n % 2 == 0:
                        for m, rows in enumerate(halves):
                            do(TTn(tile(qb[m], j)[rows, 0:S], rope[0][rows, :], rope[1][rows, :], ADD))
                        step.settle()
                    else:
                        link(TTn(tile(kb, j)[:, 0:S], rope[0], rope[1], ADD))
                    dve.sem_inc(qk_done, 1)

                for n in range(2 * JT):
                    normed(n)
                    if n >= 1:
                        rotated(n - 1)
                rotated(2 * JT - 1)
                for j in range(JT):
                    silu_of(f"ag{j}", tile(gsb, j), zc[j % 2])
                dve.wait_ge(lam_exp, 1)
                link(TTn(dcol("neglam"), dcol("ls", 3), dcol("ls", 2), SUB))
                link(TTn(dcol("neglam"), dcol("neglam"), pcol("laminit"), SUB))
                units = [(hd_, q) for hd_ in range(HEADS) for q in range(NT)]

                def maxima(u):
                    hd_, q = units[u]
                    w = T if q < 4 else P
                    st = stat[:, 8 * (u % 2):8 * (u % 2) + 8]
                    dve.wait_ge(s_full, u + 1)
                    V.tensor_reduce(st[:, 0:2], t3(ps[:, 1536 * (u % 2):1536 * (u % 2) + 2 * w], w), AX.X, ALU.max, negate=True).then_inc(s_max, 1)

                def combine(u):
                    hd_, q = units[u]
                    w = T if q < 4 else P
                    st = stat[:, 8 * (u % 2):8 * (u % 2) + 8]
                    dve.wait_ge(e_ready, u + 1)
                    link(V.reciprocal(st[:, 4:6], st[:, 2:4]))
                    link(TTn(st[:, 6:7], st[:, 5:6], dcol("neglam"), MUL))
                    if u >= 2:
                        dve.wait_ge(pT2_full, u - 1)
                    link(TS(pd[u % 2][:, 0:w], eb[u % 2][:, T:T + w], st[:, 6:7], None, MUL))
                    STT(pd[u % 2][:, 0:w], eb[u % 2][:, 0:w], st[:, 4:5], pd[u % 2][:, 0:w], MUL, ADD).then_inc(pd_ready, 1)

                maxima(0)
                for u in range(len(units)):
                    if u + 1 < len(units):
                        maxima(u + 1)
                    combine(u)
                def head_normed(hd_):
                    dve.wait_ge(ort_ready, hd_ + 1)
                    link(V.reciprocal(rr[hd_ % 2], rr[hd_ % 2]))
                    link(STT(zn[0], tile(yc, hd_), dcol("gsl"), rr[hd_ % 2], MUL, MUL))
                    dve.sem_inc(onorm_done, 1)
                    link(STT(tile(yc, hd_), zn[0], 0.5, tile(gsb, hd_), MUL, MUL))

                taps("wl", tw, dcol("hmu", 12), dcol("hmu", 12))
                dve.sem_inc(tw_lin, 1)
                head_normed(0)
                head_normed(1)
                taps("al", tal, dcol("hmu", 13), dcol("hmu", 13))
                dve.sem_inc(al_ready, 1)
                for hd_ in range(2, HEADS):
                    head_normed(hd_)
                dve.wait_ge(kv_stored, l * 32 + 32)
                dve.sem_inc(dve_phase, 1)

                E, Em = tC[2], tC[1]

                def per_chunk(ap, i):
                    return t3(ap, 128)[:, :, i:i + 1].to_broadcast([128, NT, 128])

                n_doubled = [0]

                def level_mask(name, b, s):
                    m = halves(con(f"{name}{b}").bitcast(I32), b, s)
                    return m.to_broadcast([128, NT] + list(m.shape[2:]))

                def centred(j):
                    dve.wait_ge(mu_full, j + 1)
                    do(STT(tC[0], wide(6), -1.0 / 64, tile(yb, j), MUL, ADD))
                    link(TTn(tC[3], wide(4), v_, MUL))
                    dve.sem_inc(mu_sub, 1)

                def normed_heads(j):
                    dve.wait_ge(grt_ready, j + 1)
                    link(V.reciprocal(tC[2], tC[2]))
                    link(STT(tC[4], tC[0], pcol("lnw", j), tC[2], MUL, MUL))
                    link(STT(tC[4], tC[4], pcol("lnb", j), tC[3], ADD, ADD))
                    link(STT(tile(yb, j), tC[4], 0.5, gs, MUL, MUL))
                    dve.sem_inc(yb_ready, 1)

                ar = AR.rearrange("p (a s n) -> p a s n", s=2, n=128)

                def decay(g, n):
                    j, d = g // 2, g % 2
                    u, a = ((tC[0], tC[5]), th1)[d]
                    if n == 0:
                        dve.wait_ge(th_ready, g + 1)
                        link(TS(u, u, 1.0, None, ADD))
                        link(V.tensor_tensor_scan(tC[3], resetm[:, :], u, 0.0, MUL, ADD))
                    if n == 1:
                        link(TTn(t3(E, 128), t3(tC[3], 128), per_chunk(tC[3], 63), SUB))
                        link(TTn(Em, E, u, SUB))
                        dve.sem_inc(E_ready, 1)
                    if n == 2:
                        do(STT(Bt, a, 1.0, kkb, ADD, MUL))
                        link(TS(a, a, dcol("hka", j), dcol("omka", j), MUL, ADD))
                    if n == 3:
                        link(TTn(Kt, a, k_, MUL))
                        if d == 0:
                            do(V.tensor_copy(kmix, Kt))
                        else:
                            link(TTn(kmix, kmix, Kt, ADD))
                            do(STT(tC[5], r_, dcol("rkh", j), kmix, MUL, MUL))
                    if n == 4:
                        dve.wait_ge(ex_ready, 3 * g + 1)
                        link(STT(Bt, Bt, 0.5, tC[0], MUL, MUL))
                    if n == 5:
                        link(TTn(Kt, Kt, tC[0], MUL))
                        dve.sem_inc(BK_ready, 1)

                def decay_rk(g):
                    dve.wait_ge(ex_ready, 3 * g + 2)
                    do(TTn(ar[:, :, 1, :], t3(r_, 128), t3(tC[3], 128), MUL))
                    dve.wait_ge(ex_ready, 3 * g + 3)
                    link(STT(ar[:, :, 0, :], t3(kkb, 128), -1.0, t3(tC[4], 128), MUL, MUL))
                    dc = dec[g % 2]
                    link(TTn(dc[:, 10:14], dc[:, 0:4], dc[:, 6:10], MUL))
                    dve.sem_inc(AR_ready, 1)

                for j in range(JT):
                    taps(f"rk{j}", k_, dcol("hmu", 4 + j), dcol("hmu", 4 + j))
                    dve.sem_inc(k_ready, 1)
                    if j >= 1:
                        centred(j - 1)
                    taps(f"rr{j}", r_, dcol("hmu", j), dcol("hmu", j))
                    if j >= 1:
                        normed_heads(j - 1)
                    dve.wait_ge(kk_rt, j + 1)
                    link(V.reciprocal(kkrt, kkrt))
                    link(STT(kkb, k_, pcol("kk", j), kkrt, MUL, MUL))
                    taps(f"rv{j}", v_, dcol("hmu", 8 + j), dcol("hmu", 8 + j))
                    dve.sem_inc(v_ready, 1)
                    for n in range(6):
                        decay(2 * j, n)
                    decay_rk(2 * j)
                    silu_of(f"rg{j}", gs, gth)
                    for d in range(2):
                        g = 2 * j + d
                        dc = dec[d]
                        if d == 1:
                            dve.wait_ge(Yt_full, g)
                            decay_rk(g)
                        msk = con(("mfwd", "mbwd")[d])
                        lo, up = ("lo", "up") if d == 0 else ("up", "lo")
                        for hh in range(2):
                            n = 6 * g + 3 * hh
                            dve.wait_ge(A_full, n + 1)
                            link(TTn(t3(ABQ[hh], 256), t3(ps[:, 0:2 * T], 256), over_chunks(msk), MUL))
                            dve.sem_inc(A_read, 1)
                            dve.wait_ge(A_full, n + 2)
                            link(TTn(t3(AKQ[hh], 256), t3(ps[:, 1536:1536 + 2 * T], 256), over_chunks(msk), MUL))
                            dve.sem_inc(A_read, 1)
                            dve.wait_ge(A_full, n + 3)
                            if hh == 0:
                                dve.wait_ge(ones_ready, 4 * g + 4)
                            link(V.copy_predicated(halves(Tm[hh], 1, d), level_mask(lo, 1, d), halves(wide(6), 1, d)))
                            dve.sem_inc(A_read, 1)
                            dve.sem_inc(T_ready, 1)
                            ab = ABQ[hh].rearrange("p (c z q s b) -> p c z q s b", z=2, q=64, s=2, b=1)[:, :, 0, :, 1 - d, :]
                            link(V.copy_predicated(halves(TT[hh], 1, 1 - d), level_mask(up, 1, 1 - d), ab))
                            dve.sem_inc(TT_ready, 1)
                        for lev in range(6):
                            b = LEVELS[lev + 1]
                            for part in (0, 1) if lev < 5 else (1,):
                                s = (d, 1 - d)[part]
                                for hh in range(2):
                                    n_doubled[0] += 1
                                    dve.wait_ge(D_full, n_doubled[0])
                                    link(V.copy_predicated(halves((Tm, TT)[part][hh], b, s), level_mask((lo, up)[part], b, s),
                                                           halves(wide(4 * hh + 2 - 2 * part), b, s)))
                                    dve.sem_inc((T_ready, TT_ready)[part], 1)
                            if d == 0:
                                decay(g + 1, lev)
                        dve.wait_ge(s0_in[g % 2], l * (16 * JT) + 16 * (g // 2 + 1))
                        order = [4] + ([0, 1, 2, 3] if d == 0 else [3, 2, 1, 0])
                        dve.sem_inc(M_ready, 1)
                        for n, c in enumerate(order):
                            ns = 5 * g + n
                            dve.wait_ge(U2_full, ns + 1)
                            V.tensor_copy(Us[n % 2], ps[:, 1536:1664]).then_inc(U2_ready, 1)
                            if n < 4:
                                dve.wait_ge(M_full, 4 * g + n + 1)
                            if n == 0:
                                if g >= 2:
                                    dve.wait_ge(fin_stored[g % 2], l * (16 * JT) + 16 * (g // 2))
                                do(TS(Fin[g % 2], ps[:, 1024:1088], dc[:, 4 + 5 * d:5 + 5 * d], None, MUL))
                                o = 5 if d == 0 else 3
                                link(TS(Ms[1], S0[g % 2], dc[:, o:o + 1], None, MUL))
                                dve.sem_inc(M_ready, 1)
                            elif n < 4:
                                o = 10 + (c if d == 0 else c - 1)
                                link(TS(Ms[(n + 1) % 2], ps[:, 1024:1088], dc[:, o:o + 1], None, MUL))
                                dve.sem_inc(M_ready, 1)
                        dve.sem_inc(fin_ready, 1)
                        if d == 1:
                            dve.wait_ge(Yt_full, g + 1)
                            link(TTn(tile(yb, j), tile(yb, j), wide(4), ADD))
                            dve.sem_inc(Yt_read, 1)
                centred(JT - 1)
                normed_heads(JT - 1)

                for n in range(3 * KD):
                    p, b, jj = n // 6, n // 2 % 3, n % 2
                    dve.wait_ge(tanh_ready, 3 * JT + n + 1)
                    if jj == 0:
                        dve.wait_ge(br_full, n // 2 + 1)
                    else:
                        dve.wait_ge(w_used, l * NSLOT + used(("br", p, b)))
                    dst = tile(mg, 2 * p + jj)
                    link(STT(dst if b == 0 else tD[jj], tg[n % 2], 1.0, wide(4 + 2 * jj), ADD, MUL))
                    dve.sem_inc(br_read, 1)
                    if b:
                        link(TTn(dst, dst, tD[jj], ADD))
                    if b == 2:
                        dve.sem_inc(merged_ready, 1)
                for j in range(KD):
                    dve.wait_ge(w_used, l * NSLOT + used(("out", j)))
                    z = wide(4 + 2 * (j % 2))
                    for s, (lo_, hi_) in enumerate(((0, S), (S, T))):
                        do(STT(xt(j)[:, lo_:hi_], z[:, lo_:hi_], dcol("gate", 2 * j + s), xt(j)[:, lo_:hi_], MUL, ADD))
                    step.settle()
                    dve.sem_inc(out_read, 1)
                dve.wait_ge(layer_over, 3)
                dve.sem_clear(range(first, last + 1))
                dve.sem_inc(x_ready, 1)


def _tables():
    c = np.zeros((128, NCONST), np.float32)

    def put(name, a, row=0):
        o, w = CCOL[name]
        c[row:row + a.shape[0], o:o + a.shape[1]] = a

    i = np.arange(128)
    put("ident", np.eye(128))
    put("ones", np.ones((128, 128)))
    put("bones", (i[:, None] // 64 == i[None, :] // 64).astype(np.float32))
    rot = np.zeros((128, 128))
    for m in range(128):
        if m % 32 < 16:
            rot[m + 16, m] = -1.0
        else:
            rot[m - 16, m] = 1.0
    put("rot", rot)
    freqs = (10000.0 ** (-np.arange(16, dtype=np.float32) / np.float32(16))).astype(np.float32)
    t = np.arange(S)
    pos = np.where((i % 64)[:, None] < 32, (t // GRID_W)[None, :], (t % GRID_W)[None, :]).astype(np.float32)
    ang = (pos * freqs[i % 16][:, None]).astype(np.float64)
    put("cos", np.cos(ang))
    put("sin", np.sin(ang))
    feats, wins = [], []
    deltas = np.abs(np.linspace(math.log(1e-2) / 1.5, math.log(1e-2) / 0.3, BR))
    bands = np.linspace(1e-4, 15, 16)[:, None]
    for L in (S, P):
        tl = np.linspace(0.0, 1.0, L)
        w = 2.0 * math.pi * np.arange(L)[None, :] / L
        feats.append(np.concatenate([tl[None, :], np.cos(bands * w), -np.sin(bands * w)], 0))
        wins.append(np.exp(-tl[:, None] * deltas[None, :]))
    put("feat", np.concatenate(feats, 1), 64)
    up, upi = (i[:, None] < i[None, :]), (i[:, None] <= i[None, :])
    put("mfwd", np.concatenate([up, upi], 1))
    put("mbwd", np.concatenate([up.T, upi.T], 1))
    put("eps", np.tile([[1e-6, 1e-12, 64e-5, 1e-5]], (128, 1)))
    for b in LEVELS:
        lo = ((i[:, None] // b) % 2 == 1) & (i[None, :] // b == i[:, None] // b - 1)
        put(f"lo{b}", lo)
        put(f"up{b}", lo.T)
    win = np.concatenate(wins, 0).reshape(NT, 128, BR).transpose(1, 0, 2).reshape(128, NT * BR)
    tab, inv = [], []
    for L in (S, P):
        om = 2.0 * math.pi * (np.arange(L) + 0.5) / (2 * L)
        a = np.arange(L)[:, None] * om[None, :]
        for f in range(L // 128):
            for fn in (np.cos, np.sin):
                tab.append(fn(a[:, f * 128:(f + 1) * 128]).reshape(L // 128, 128, 128).transpose(1, 0, 2).reshape(128, L))
                inv.append(fn(a[:, f * 128:(f + 1) * 128]).T / L)
    f32 = np.float32
    return c, win.astype(f32), np.concatenate(tab, 1).astype(f32), np.concatenate(inv, 1).astype(f32)


def _pack(v):
    f32 = np.float32
    cst, win, tab, inv = _tables()
    o = CCOL["c"][0]
    cst[:, o:o + 16:2] = v["c"].reshape(KD, 128).T
    cst[:, o + 1:o + 16:2] = v["c_ctx"].reshape(KD, 128).T
    w = np.zeros((DEPTH, NSLOT, 128, 1024), f32)
    par = np.zeros((DEPTH, 128, NPAR), f32)
    for l in range(DEPTH):
        def col_tile(m, o):
            return m[:, o:o + 128].reshape(-1, 128, 128).transpose(1, 0, 2).reshape(128, -1)

        for i, key in enumerate(ORDER):
            if key[0] == "z":
                w[l, i] = col_tile(v["w_in"][l], ZSRC[key[1]])
            elif key[0] == "out":
                w[l, i] = col_tile(v["w_out"][l], 128 * key[1])
            elif key[0] == "br":
                w[l, i] = np.concatenate([col_tile(v["w_br"][l, key[2]], 128 * (2 * key[1] + jj)) for jj in range(2)], 1)
            elif key[0] == "ada":
                a = v["w_ada"][l][256 * key[2]:256 * (key[2] + 1), 512 * key[1]:512 * (key[1] + 1)]
                w[l, i] = a.reshape(2, 128, 512).transpose(1, 0, 2).reshape(128, 1024)
            elif key[0] == "filt":
                w[l, i, 0:64] = v["hy_f3"][l]
                w[l, i, 64:128, 0:64] = v["hy_f2"][l]
                w[l, i, 64:64 + HY_EMB, 64:128] = v["hy_f1"][l]
            else:
                w[l, i, :, 0:512] = v["rw_w2"][l].reshape(128, 512)
                w[l, i, :, 512:1024] = v["rw_a2"][l].reshape(128, 512)

        def put(name, a):
            o, n = PCOL[name]
            par[l, :, o:o + n] = a

        def cols(a):
            return np.asarray(a).reshape(-1, 128).T

        put("g", cols(v["norm_g"][l]))
        put("bada", cols(v["b_ada"][l]))
        for n in range(3):
            put(f"cw{n}", cols(v["hy_conv_w"][l, n]))
        put("cb", cols(v["hy_conv_b"][l]))
        put("hyb", cols(v["hy_bias"][l]))
        for name, key in (("mu", "rw_mu"), ("w0", "rw_w0"), ("a0", "rw_a0"), ("kk", "rw_kk"), ("ka", "rw_ka"),
                          ("rk", "rw_rk"), ("lnw", "rw_ln_w"), ("lnb", "rw_ln_b"), ("gsub", "da_gsub")):
            put(name, cols(v[key][l]))
        put("gq", np.tile(v["da_gq"][l], 2)[:, None])
        put("gk", np.tile(v["da_gk"][l], 2)[:, None])
        put("fb", np.concatenate([v["hy_fb2"][l], v["hy_fb1"][l]])[:, None])
        put("freq", np.tile(v["hy_freq"][l], 2)[:, None])
        lam = 0.8 - 0.6 * math.exp(-0.3 * l)
        put("laminit", np.full((128, 1), lam, f32))
        put("oneml", np.full((128, 1), 1.0 - lam, f32))
        for name in ("lq1", "lk1", "lq2", "lk2"):
            put(name, np.broadcast_to(v[f"da_{name}"][l], (128, 64)))
    xt = np.concatenate([v["x_sample"][0], v["x_prompt"][0]], 0).T
    s0 = v["state_rwkv"][0].reshape(DEPTH, 2, JT, 2, 64, 64).transpose(0, 3, 5, 2, 1, 4)
    return {
        "w": w.reshape(DEPTH * NSLOT, 128, 1024), "par": par, "cst": cst, "win": win, "tab": tab, "inv": inv,
        "x": xt.reshape(KD, 128, T).transpose(1, 0, 2).reshape(128, KD * T),
        "ck": v["cache_k"][0].transpose(0, 3, 4, 2, 1).reshape(DEPTH, 128, HEADS * PAST),
        "cv": v["cache_v"][0].reshape(DEPTH, PAST, BR),
        "s0": s0.reshape(DEPTH, 128, 512),
    }


def kernel(**inputs):
    import numpy as _np
    import concourse.bacc as _bacc
    from concourse.bass_utils import run_bass_kernel_spmd as _run

    arrays = {k: _np.ascontiguousarray(a) for k, a in _pack({k: _np.asarray(a) for k, a in inputs.items()}).items()}
    outs = {"y": (128, KD * T), "new_k": (DEPTH, 128, HEADS * P), "new_v": (DEPTH, P, BR), "new_s": (DEPTH, 128, 512)}
    nc = _bacc.Bacc("TRN2", target_bir_lowering=False, num_devices=1)
    args = {k: nc.dram_tensor(f"in_{k}", a.shape, F32, kind="ExternalInput").ap() for k, a in arrays.items()}
    args.update({k: nc.dram_tensor(f"out_{k}", s, F32, kind="ExternalOutput").ap() for k, s in outs.items()})
    build(nc, args)
    r = _run(nc, [{f"in_{k}": a for k, a in arrays.items()}], core_ids=[0]).results[0]
    y = _np.asarray(r["out_y"]).reshape(128, KD, T).transpose(2, 1, 0).reshape(T, D)
    new_k = _np.asarray(r["out_new_k"]).reshape(DEPTH, 2, DH, HEADS, P).transpose(0, 4, 3, 1, 2)[None]
    new_v = _np.asarray(r["out_new_v"]).reshape(DEPTH, P, HEADS, 2 * DH)[None]
    new_s = _np.asarray(r["out_new_s"]).reshape(DEPTH, 2, 64, JT, 2, 64).transpose(0, 4, 3, 1, 5, 2).reshape(1, DEPTH, 2, 8, 64, 64)
    c = _np.ascontiguousarray
    return c(y[None, S:T]), c(y[None, 0:S]), c(new_k), c(new_v), c(new_s)
```
